# Optimizing a Trainium2 kernel written in Bass

```python
import math
import jax
import jax.numpy as jnp
from jax import lax
import numpy as np

D_MODEL = 1024
BATCH = 1
SEQ = 256
DEPTH = 2

N_A_LAYERS = DEPTH // 2
N_B_LAYERS = DEPTH - N_A_LAYERS
N_DENSE_LAYERS = (DEPTH + 1) // 2
N_MOE_LAYERS = DEPTH // 2

HGRN_EXPAND = 128
HGRN_HEADS = D_MODEL // HGRN_EXPAND
HGRN_DK = HGRN_EXPAND
HGRN_DV = D_MODEL // HGRN_HEADS
HGRN_CHUNK = 64

SWA_HEAD_DIM = 64
SWA_Q_HEADS = D_MODEL // SWA_HEAD_DIM
SWA_KV_HEADS = 4
SWA_GROUP = SWA_Q_HEADS // SWA_KV_HEADS
WINDOW = 128

REL_BUCKETS = 32
REL_MAX_DIST = 128

D_FF_DENSE = 2816
N_EXPERTS = 8
TOP_K = 2
D_FF_EXPERT = 3584
MOE_BLOCK = 256

NORM_EPS = 1e-6

kernel_name = 'hybrid_hgrn2_swa_yoco_moe'

def rmsnorm(x, gain):
    xf = x.astype(jnp.float32)
    y = xf * lax.rsqrt(jnp.mean(xf * xf, axis=-1, keepdims=True) + NORM_EPS)
    return (y * gain.astype(jnp.float32)).astype(x.dtype)

def hgrn2_mixer(hn, w_in, lb, g_norm, w_out):
    B, S, _ = hn.shape
    nc = S // HGRN_CHUNK
    proj = hn @ w_in
    q, f_raw, i_in, o_gate = jnp.split(proj, 4, axis=-1)
    lbf = lb.astype(jnp.float32)
    f = lbf + (1.0 - lbf) * jax.nn.sigmoid(f_raw.astype(jnp.float32))
    log_f = jnp.log(f)
    k = 1.0 - f

    def to_chunks(t, d):
        return t.astype(jnp.float32).reshape(B, nc, HGRN_CHUNK, HGRN_HEADS, d).transpose(1, 0, 3, 2, 4)

    qc = to_chunks(q, HGRN_DK)
    kc = to_chunks(k, HGRN_DK)
    vc = to_chunks(i_in, HGRN_DV)
    gc = to_chunks(log_f, HGRN_DK)
    causal = jnp.tril(jnp.ones((HGRN_CHUNK, HGRN_CHUNK), dtype=bool))

    def chunk_step(state, inp):
        qt, kt, vt, gt = inp
        b = jnp.cumsum(gt, axis=2)
        rel = b[:, :, :, None, :] - b[:, :, None, :, :]
        decay = jnp.exp(jnp.where(causal[:, :, None], rel, -jnp.inf))
        scores = jnp.einsum('bhtd,bhsd,bhtsd->bhts', qt, kt, decay)
        o = scores @ vt + jnp.einsum('bhtd,bhde->bhte', qt * jnp.exp(b), state)
        b_last = b[:, :, -1:, :]
        new_state = jnp.exp(b_last[:, :, 0, :])[..., None] * state + jnp.einsum(
            'bhsd,bhse->bhde', kt * jnp.exp(b_last - b), vt)
        return new_state, o

    s0 = jnp.zeros((B, HGRN_HEADS, HGRN_DK, HGRN_DV), jnp.float32)
    _, o = lax.scan(chunk_step, s0, (qc, kc, vc, gc))
    o = o.transpose(1, 0, 3, 2, 4).reshape(B, S, HGRN_HEADS, HGRN_DV)
    o = rmsnorm(o, g_norm).reshape(B, S, HGRN_HEADS * HGRN_DV)
    o = o * jax.nn.silu(o_gate.astype(jnp.float32))
    return o.astype(hn.dtype) @ w_out

def shared_kv(h, kv_norm, kv_w, k_gain):
    B, S, _ = h.shape
    nb = S // WINDOW
    hn = rmsnorm(h, kv_norm)
    kv = hn @ kv_w
    k, v = jnp.split(kv, 2, axis=-1)
    k = rmsnorm(k.reshape(B, S, SWA_KV_HEADS, SWA_HEAD_DIM), k_gain)
    v = v.reshape(B, S, SWA_KV_HEADS, SWA_HEAD_DIM)

    def band(t):
        tp = jnp.pad(t.astype(jnp.float32), ((0, 0), (WINDOW, 0), (0, 0), (0, 0)))
        tb = tp.reshape(B, nb + 1, WINDOW, SWA_KV_HEADS, SWA_HEAD_DIM)
        return jnp.concatenate([tb[:, :-1], tb[:, 1:]], axis=2)

    return band(k), band(v)

def rel_bucket(n):
    max_exact = REL_BUCKETS // 2
    nf = jnp.maximum(n, 1).astype(jnp.float32)
    large = max_exact + (jnp.log(nf / max_exact) / math.log(REL_MAX_DIST / max_exact)
                         * (REL_BUCKETS - max_exact)).astype(jnp.int32)
    large = jnp.minimum(large, REL_BUCKETS - 1)
    return jnp.where(n < max_exact, n, large)

def swa_attention(hn, k_band, v_band, w_q, q_gain, sink, rel_bias, w_o):
    B, S, _ = hn.shape
    nb = S // WINDOW
    q = (hn @ w_q).reshape(B, S, SWA_Q_HEADS, SWA_HEAD_DIM)
    q = rmsnorm(q, q_gain)
    qb = q.astype(jnp.float32).reshape(B, nb, WINDOW, SWA_KV_HEADS, SWA_GROUP, SWA_HEAD_DIM)
    scores = jnp.einsum('bnqkgd,bnskd->bnkgqs', qb, k_band) * (SWA_HEAD_DIM ** -0.5)
    qi = jnp.arange(WINDOW)[:, None]
    kj = jnp.arange(2 * WINDOW)[None, :]
    dist = qi + WINDOW - kj
    in_win = (dist >= 0) & (dist < WINDOW)
    bias = rel_bias.astype(jnp.float32)[rel_bucket(jnp.maximum(dist, 0))]
    bias = bias.transpose(2, 0, 1).reshape(SWA_KV_HEADS, SWA_GROUP, WINDOW, 2 * WINDOW)
    first_ok = (jnp.arange(nb)[:, None] > 0) | (jnp.arange(2 * WINDOW)[None, :] >= WINDOW)
    valid = in_win[None, :, :] & first_ok[:, None, :]
    logits = jnp.where(valid[None, :, None, None], scores + bias, -jnp.inf)
    sink_l = sink.astype(jnp.float32).reshape(SWA_KV_HEADS, SWA_GROUP)[None, None, :, :, None, None]
    m = jnp.maximum(jnp.max(logits, axis=-1, keepdims=True), sink_l)
    p = jnp.exp(logits - m)
    probs = p / (jnp.sum(p, axis=-1, keepdims=True) + jnp.exp(sink_l - m))
    out = jnp.einsum('bnkgqs,bnskd->bnqkgd', probs, v_band).reshape(B, S, SWA_Q_HEADS * SWA_HEAD_DIM)
    return out.astype(hn.dtype) @ w_o

def swiglu(hn, w_gate, w_up, w_down):
    return (jax.nn.silu(hn @ w_gate) * (hn @ w_up)) @ w_down

def moe_swiglu(hn, w_router, w_gate, w_up, w_down):
    B, S, D = hn.shape
    T = B * S
    A = T * TOP_K
    xt = hn.reshape(T, D)
    logits = (xt @ w_router).astype(jnp.float32)
    top_logit, top_idx = lax.top_k(logits, TOP_K)
    gates = jax.nn.softmax(top_logit, axis=-1)
    flat_e = top_idx.reshape(A)
    flat_tok = jnp.repeat(jnp.arange(T, dtype=jnp.int32), TOP_K)
    flat_g = gates.reshape(A)
    order = jnp.argsort(flat_e, stable=True)
    s_e = flat_e[order]
    s_tok = flat_tok[order]
    s_g = flat_g[order]
    counts = jnp.bincount(flat_e, length=N_EXPERTS)
    padded = (counts + MOE_BLOCK - 1) // MOE_BLOCK * MOE_BLOCK
    pad_end = jnp.cumsum(padded)
    pad_start = pad_end - padded
    grp_start = jnp.cumsum(counts) - counts
    dest = pad_start[s_e] + jnp.arange(A) - grp_start[s_e]
    m_pad = A + N_EXPERTS * MOE_BLOCK
    n_blk = m_pad // MOE_BLOCK
    row_tok = jnp.zeros((m_pad,), jnp.int32).at[dest].set(s_tok)
    row_g = jnp.zeros((m_pad,), jnp.float32).at[dest].set(s_g)
    blk_e = jnp.minimum(jnp.searchsorted(pad_end, jnp.arange(n_blk) * MOE_BLOCK, side='right'),
                        N_EXPERTS - 1)
    xs = xt[row_tok].reshape(n_blk, MOE_BLOCK, D)

    def expert_block(args):
        xb, e = args
        hid = jax.nn.silu(xb @ w_gate[e]) * (xb @ w_up[e])
        return hid @ w_down[e]

    yb = lax.map(expert_block, (xs, blk_e)).reshape(m_pad, D)
    y = jnp.zeros((T, D), hn.dtype).at[row_tok].add(
        (yb.astype(jnp.float32) * row_g[:, None]).astype(hn.dtype))
    return y.reshape(B, S, D)

def setup_inputs(seed: int = 0) -> dict:
    key = jax.random.key(seed)
    ks = jax.random.split(key, 24)
    D = D_MODEL
    f32 = jnp.float32

    def w(k, shape, fan_in):
        return jax.random.normal(k, shape, f32) * (fan_in ** -0.5)

    def gain(k, shape):
        return 1.0 + 0.05 * jax.random.normal(k, shape, f32)

    q_width = SWA_Q_HEADS * SWA_HEAD_DIM
    kv_width = 2 * SWA_KV_HEADS * SWA_HEAD_DIM
    return {
        'x': jax.random.normal(ks[0], (BATCH, SEQ, D), f32),
        'hgrn_w_in': w(ks[1], (N_A_LAYERS, D, 4 * D), D),
        'hgrn_lb': 0.1 * jax.random.normal(ks[2], (DEPTH + 1, D), f32),
        'hgrn_gnorm': gain(ks[3], (N_A_LAYERS, HGRN_DV)),
        'hgrn_w_out': w(ks[4], (N_A_LAYERS, D, D), D),
        'swa_w_q': w(ks[5], (N_B_LAYERS, D, q_width), D),
        'swa_q_gain': gain(ks[6], (N_B_LAYERS, SWA_HEAD_DIM)),
        'swa_sink': jax.random.normal(ks[7], (N_B_LAYERS, SWA_Q_HEADS), f32),
        'swa_w_o': w(ks[8], (N_B_LAYERS, q_width, D), q_width),
        'kv_norm': gain(ks[9], (D,)),
        'kv_w': w(ks[10], (D, kv_width), D),
        'k_gain': gain(ks[11], (SWA_HEAD_DIM,)),
        'rel_bias': 0.5 * jax.random.normal(ks[12], (REL_BUCKETS, SWA_Q_HEADS), f32),
        'attn_norm': gain(ks[13], (DEPTH, D)),
        'ffn_norm': gain(ks[14], (DEPTH, D)),
        'ffn_w_gate': w(ks[15], (N_DENSE_LAYERS, D, D_FF_DENSE), D),
        'ffn_w_up': w(ks[16], (N_DENSE_LAYERS, D, D_FF_DENSE), D),
        'ffn_w_down': w(ks[17], (N_DENSE_LAYERS, D_FF_DENSE, D), D_FF_DENSE),
        'moe_router': w(ks[18], (N_MOE_LAYERS, D, N_EXPERTS), D),
        'moe_w_gate': w(ks[19], (N_MOE_LAYERS, N_EXPERTS, D, D_FF_EXPERT), D),
        'moe_w_up': w(ks[20], (N_MOE_LAYERS, N_EXPERTS, D, D_FF_EXPERT), D),
        'moe_w_down': w(ks[21], (N_MOE_LAYERS, N_EXPERTS, D_FF_EXPERT, D), D_FF_EXPERT),
    }

def reference(x, hgrn_w_in, hgrn_lb, hgrn_gnorm, hgrn_w_out, swa_w_q, swa_q_gain, swa_sink,
              swa_w_o, kv_norm, kv_w, k_gain, rel_bias, attn_norm, ffn_norm, ffn_w_gate,
              ffn_w_up, ffn_w_down, moe_router, moe_w_gate, moe_w_up, moe_w_down):
    h = x
    lb_all = jnp.cumsum(jax.nn.softmax(hgrn_lb.astype(jnp.float32), axis=0), axis=0)
    k_band = None
    v_band = None
    for l in range(DEPTH):
        hn = rmsnorm(h, attn_norm[l])
        if l < N_A_LAYERS:
            a = l
            h = h + hgrn2_mixer(hn, hgrn_w_in[a], lb_all[l], hgrn_gnorm[a], hgrn_w_out[a])
        else:
            bi = l - N_A_LAYERS
            h = h + swa_attention(hn, k_band, v_band, swa_w_q[bi], swa_q_gain[bi], swa_sink[bi],
                                  rel_bias, swa_w_o[bi])
        hn = rmsnorm(h, ffn_norm[l])
        if l % 2 == 0:
            h = h + swiglu(hn, ffn_w_gate[l // 2], ffn_w_up[l // 2], ffn_w_down[l // 2])
        else:
            h = h + moe_swiglu(hn, moe_router[l // 2], moe_w_gate[l // 2], moe_w_up[l // 2],
                               moe_w_down[l // 2])
        if l == N_A_LAYERS - 1:
            k_band, v_band = shared_kv(h, kv_norm, kv_w, k_gain)
    return h


_drawn_inputs = setup_inputs


def setup_inputs(seed=0):
    import zlib

    import numpy as np

    out = dict(_drawn_inputs(seed))
    spreads = {}
    factors = {}
    for name, (base, spread) in spreads.items():
        noise = np.random.default_rng([zlib.crc32(name.encode()), seed]).standard_normal(out[name].shape)
        drawn = base * np.exp(spread * noise) if base else spread * noise
        out[name] = jnp.asarray(drawn.astype(out[name].dtype))
    for name, factor in factors.items():
        out[name] = (out[name] * factor).astype(out[name].dtype)
    return out
```

```python
import math
from contextlib import ExitStack

import numpy as np
import concourse.bass as bass
from concourse import mybir

P = 128
D = 1024
KT = D // P
T = 256
TT = T // P
HEADS, HD = 8, 128
CH = 64
NCH = T // CH
QH, KVH, AD = 16, 4, 64
GRP = QH // KVH
WIN = 128
BUCKETS, MAX_DIST = 32, 128
FF = 2816
E, FE = 8, 3584
FKT = FE // P
EPS = 1e-6
MASKED = -1e30

CW = 2048
RAW, SPLIT = 6, 3
LEAD = 2
N_IN, N_OUT, N_FF, N_DOWN, N_KV, N_Q, N_O = 16, 4, 2 * FF // 256, FF // 256, 2, 4, 4
C_OUT = N_IN
C_FF = C_OUT + N_OUT
C_DOWN = C_FF + N_FF
C_KV = C_DOWN + N_DOWN
C_Q = C_KV + N_KV
C_O = C_Q + N_Q
C_MOE = C_O + N_O
BLK = FE // 512
N_UP = 4 * BLK
N_ITEM = N_UP + FKT // 2
AHEAD = RAW
MAX_ITEMS = 11

K_ID, K_ANTI, K_TRI, K_STRICT, K_IOTA, K_HOT, K_MASK, K_END = 0, 128, 256, 640, 768, 896, 1280, 1664


def shape_constants():
    c = np.zeros((P, K_END), np.float32)
    r = np.arange(P)
    c[:, K_ID:K_ID + P] = r[:, None] == r[None]
    c[:, K_ANTI:K_ANTI + P] = r[:, None] + r[None] == P - 1
    upper = r[:, None] <= r[None]
    c[:, K_TRI:K_TRI + P] = upper
    c[:, K_TRI + P:K_TRI + 2 * P] = upper
    c[:, K_TRI + 2 * P:K_TRI + 3 * P] = 1.0
    c[:, K_STRICT:K_STRICT + P] = r[:, None] < r[None]
    c[:, K_IOTA:K_IOTA + P] = r[None]
    exact = BUCKETS // 2
    for m in range(3 * P):
        dist = 2 * P - 1 - m
        if 0 <= dist < WIN:
            b = dist
            if dist >= exact:
                f = np.log(np.float32(dist) / np.float32(exact)) / np.float32(math.log(MAX_DIST / exact))
                b = min(exact + int(np.float32(f) * np.float32(BUCKETS - exact)), BUCKETS - 1)
            c[b, K_HOT + m] = 1.0
        else:
            c[:, K_MASK + m] = MASKED
    return c


def build_program(nc, a, out):
    f32, f32r = mybir.dt.float32, mybir.dt.float32r
    i32, u32 = mybir.dt.int32, mybir.dt.uint32
    ALU, ACT, AX = mybir.AluOpType, mybir.ActivationFunctionType, mybir.AxisListType
    MUL, ADD, SUB = ALU.mult, ALU.add, ALU.subtract

    def plain(ap):
        return ap.bitcast(f32)

    w_in = a["hgrn_w_in"][0]
    deep = lambda w, c, n: w[:, c:c + n].rearrange("(k p) c -> p k c", p=P)
    flat = lambda w, r, n: w[r:r + n, :].rearrange("(k p) c -> p k c", p=P)
    stream = []
    for part in (1, 0, 2, 3):
        stream += [deep(w_in, part * D + 256 * i, 256) for i in range(4)]
    stream += [flat(a["hgrn_w_out"][0], 256 * i, 256) for i in range(N_OUT)]
    for b in range(FF // 256):
        stream += [deep(a["ffn_w_gate"][0], 256 * b, 256), deep(a["ffn_w_up"][0], 256 * b, 256)]
    stream += [flat(a["ffn_w_down"][0], 256 * i, 256) for i in range(N_DOWN)]
    stream += [flat(a["kv_w"], 512 * i, 512) for i in range(N_KV)]
    stream += [flat(a["swa_w_q"][0], 256 * i, 256) for i in range(N_Q)]
    stream += [flat(a["swa_w_o"][0], 256 * i, 256) for i in range(N_O)]
    assert len(stream) == C_MOE and C_MOE % SPLIT == 0 and N_ITEM % RAW == 0 and N_ITEM % SPLIT == 0

    def item_source(e, j):
        if j < N_UP:
            b, i = divmod(j, 4)
            w = a["moe_w_gate"] if i < 2 else a["moe_w_up"]
            r = 512 * (i % 2)
            return w[0][bass.ds(e, 1), r:r + 512, 512 * b:512 * b + 512].rearrange("e (k p) c -> p (e k) c", p=P)
        r = 256 * (j - N_UP)
        return a["moe_w_down"][0][bass.ds(e, 1), r:r + 256, :].rearrange("e (k p) c -> p (e k) c", p=P)

    scratch = nc.dram_tensor("bias_rows", [QH, 3 * P], f32, kind="Internal").ap()

    ctx = ExitStack()
    with ctx:
        def sb(stack, name, shape, dt=f32):
            return stack.enter_context(nc.sbuf_tensor(name, shape, dt))

        def sem(name):
            return ctx.enter_context(nc.semaphore(name))

        raw = sb(ctx, "raw", [P, RAW, CW])
        w_hi = sb(ctx, "w_hi", [P, SPLIT, CW], f32r)
        w_lo = sb(ctx, "w_lo", [P, SPLIT, CW], f32r)
        h = sb(ctx, "h", [P, TT, D])
        ht_hi = sb(ctx, "ht_hi", [P, KT, T], f32r)
        ht_lo = sb(ctx, "ht_lo", [P, KT, T], f32r)
        xs = sb(ctx, "xs", [P, TT, D])
        const = sb(ctx, "const", [P, K_END])
        vecs = sb(ctx, "vecs", [64, P])
        cols = sb(ctx, "cols", [P, 64])
        gain_row = sb(ctx, "gain_row", [P, D])
        gnorm = sb(ctx, "gnorm", [P, HD])
        qgain = sb(ctx, "qgain", [P, AD])
        kgain = sb(ctx, "kgain", [P, AD])
        sink = sb(ctx, "sink", [P, QH])
        rel = sb(ctx, "rel", [BUCKETS, QH])
        router = sb(ctx, "router", [P, KT, E])
        bias_row = sb(ctx, "bias_row", [QH, 3 * P])
        eps = sb(ctx, "eps", [P, 1])
        ssq = sb(ctx, "ssq", [P, 32])
        rstd = sb(ctx, "rstd", [P, 32])
        lb = sb(ctx, "lb", [P, 8, 8])
        items = sb(ctx, "items", [1, 32], i32)

        s = ExitStack()
        fT = sb(s, "fT", [P, HEADS, T])
        qT = sb(s, "qT", [P, HEADS, T])
        gT = sb(s, "gT", [P, HEADS, T])
        eT = sb(s, "eT", [P, HEADS, T])
        q_from = [sb(s, f"q_from{j}", [P, HEADS, NCH - 1 - j, CH]) for j in range(NCH - 1)]
        val = sb(s, "val", [P, TT, D])
        og = sb(s, "og", [P, TT, D])
        sc = sb(s, "sc", [P, 2, 3 * P])
        mid = sb(s, "mid", [P, HEADS, NCH])
        tot = sb(s, "tot", [P, HEADS, NCH])
        dec = sb(s, "dec", [P, 6, HEADS])
        s.close()
        s = ExitStack()
        mid_hi = sb(s, "mid_hi", [P, FF // P, T], f32r)
        mid_lo = sb(s, "mid_lo", [P, FF // P, T], f32r)
        ff_silu = sb(s, "ff_silu", [P, 2, 512])
        ff_hid = sb(s, "ff_hid", [P, 2, 512])
        s.close()
        s = ExitStack()
        bias_rev = sb(s, "bias_rev", [P, QH, 2 * P])
        kv_hi = sb(s, "kv_hi", [P, KT, T], f32r)
        kv_lo = sb(s, "kv_lo", [P, KT, T], f32r)
        vt = sb(s, "vt", [P, TT, 256])
        kT = sb(s, "kT", [P, 2, KVH, T])
        aqT = sb(s, "aqT", [P, QH // 2, T])
        pr = sb(s, "pr", [P, 12, P])
        pT = sb(s, "pT", [P, 12, P])
        kk = pT[:, 0:4, :].rearrange("p (t k) c -> p t (k c)", t=TT)
        ksq = pr[:, 0:4, :].rearrange("p (t k) c -> p t (k c)", t=TT)
        k2 = pr[:, 4:12, :].rearrange("p (t g) (i e) -> p t g i e", t=TT, i=2)
        mx = sb(s, "mx", [P, KVH, TT, GRP])
        negm = sb(s, "negm", [P, KVH, TT, GRP])
        sinkd = sb(s, "sinkd", [P, KVH, TT, GRP])
        rsum = sb(s, "rsum", [P, KVH, TT, GRP])
        s.close()
        s = ExitStack()
        hid_hi = sb(s, "hid_hi", [P, FKT, P], f32r)
        hid_lo = sb(s, "hid_lo", [P, FKT, P], f32r)
        hn_hi = sb(s, "hn_hi", [P, TT, D], f32r)
        hn_lo = sb(s, "hn_lo", [P, TT, D], f32r)
        sel = sb(s, "sel", [P, TT, P], f32r)
        sel1 = sb(s, "sel1", [P, TT, 2, P])
        gat1 = sb(s, "gat1", [P, TT, 2, P])
        gat = sb(s, "gat", [P, TT, P])
        gatT = sb(s, "gatT", [P, T])
        yb = sb(s, "yb", [P, D])
        pos = sb(s, "pos", [P, TT, 2])
        gate = sb(s, "gate", [P, TT, 2])
        rt = ExitStack()
        hnT = sb(rt, "hnT", [P, KT, T])
        rt.close()
        e_silu = sb(s, "e_silu", [P, 2, 512])
        e_hid = sb(s, "e_hid", [P, 2, 512])
        s.close()
        lg = sb(ctx, "lg", [P, TT, E])
        top = sb(ctx, "top", [P, TT, 8])
        topi = sb(ctx, "topi", [P, TT, 8], u32)
        topf = sb(ctx, "topf", [P, TT, 2])
        hot = sb(ctx, "hot", [P, TT, 2, E])
        mask = sb(ctx, "mask", [P, TT, E])
        rank = sb(ctx, "rank", [P, 3, E])
        r1 = sb(ctx, "r1", [P, 8, E])
        it = sb(ctx, "it", [1, 4, 8, E])
        itf = sb(ctx, "itf", [1, 32])

        banks = [ctx.enter_context(nc.psum_tensor(f"bank{i}", [P, 512], f32)) for i in range(8)]
        turn = banks[6:8]

        raw_full = [sem(f"raw_full{i}") for i in range(RAW)]
        hi_ready = sem("hi_ready")
        split_ready = sem("split_ready")
        chunk_used = sem("chunk_used")
        params_loaded = sem("params_loaded")
        x_loaded = sem("x_loaded")
        act_own = sem("act_own")
        dve_own = sem("dve_own")
        pool_own = sem("pool_own")
        turned = sem("turned")
        turn_hi = sem("turn_hi")
        turn_free = sem("turn_free")
        eps_ready = sem("eps_ready")
        rstd_ready = sem("rstd_ready")
        xs_ready = sem("xs_ready")
        bias_made = sem("bias_made")
        bias_stored = sem("bias_stored")
        bias_loaded = sem("bias_loaded")
        proj_free = sem("proj_free")
        f_ready = sem("f_ready")
        lb_logit = sem("lb_logit")
        lb_exp = sem("lb_exp")
        ln_ready = sem("ln_ready")
        rel_ready = sem("rel_ready")
        exp_ready = sem("exp_ready")
        q_scaled = sem("q_scaled")
        expk_ready = sem("expk_ready")
        dec_ready = sem("dec_ready")
        decays = sem("decays")
        hgrn_ready = sem("hgrn_ready")
        keep_ready = sem("keep_ready")
        og_ready = sem("og_ready")
        sc_full = sem("sc_full")
        sc_masked = sem("sc_masked")
        o_done = sem("o_done")
        sq_ready = sem("sq_ready")
        ssq_ready = sem("ssq_ready")
        h_ready = sem("h_ready")
        silu_ready = sem("silu_ready")
        hid_ready = sem("hid_ready")
        mid_rounded = sem("mid_rounded")
        mid_split = sem("mid_split")
        kv_out = sem("kv_out")
        logits_full = sem("logits_full")
        negm_ready = sem("negm_ready")
        exps_ready = sem("exps_ready")
        probs_ready = sem("probs_ready")
        att_full = sem("att_full")
        att_hi = sem("att_hi")
        att_split = sem("att_split")
        hn_ready = sem("hn_ready")
        hn_rounded = sem("hn_rounded")
        hn_split = sem("hn_split")
        logit_full = sem("logit_full")
        mask_ready = sem("mask_ready")
        rank_full = sem("rank_full")
        gap_ready = sem("gap_ready")
        gap_exp = sem("gap_exp")
        routed = sem("routed")
        yb_ready = sem("yb_ready")
        sel_ready = sem("sel_ready")
        stored = sem("stored")
        sp_pace = sem("sp_pace")
        pool_pace = sem("pool_pace")

        block = ctx.enter_context(nc.Block())

        def split_view(buf, c, width):
            return buf[:, c % SPLIT, :].rearrange("p (k c) -> p k c", c=width)

        TURN_ITEM = 14
        HID_TURN = [4, 5, 7, 8, 9, 10, 11]
        GAT_TURN, GATHER_TURN = 6, 12
        TURN0 = 2 + 4 + 4 + 4 + 4 + TT + 4 + 3 * KVH + 4 + 2

        @block.sync
        def _(sp):
            for c, src in enumerate(stream):
                if c >= RAW:
                    sp.wait_ge(split_ready, c - RAW + 1)
                dst = raw[:, c % RAW, :].rearrange("p (k c) -> p k c", k=src.shape[1])
                sp.dma_start(dst, src).then_inc(raw_full[c % RAW], 16)

            def load(e, j, c):
                src = item_source(e, j)
                sp.wait_ge(split_ready, c - RAW + 1)
                if not isinstance(c, int):
                    sp.sem_inc(sp_pace, 1)
                slot = (C_MOE + j) % RAW
                dst = raw[:, slot, :].rearrange("p (k c) -> p k c", k=src.shape[1])
                sp.dma_start(dst, src).then_inc(raw_full[slot], 16)

            for j in range(AHEAD):
                load(0, j, C_MOE + j)
            sp.wait_ge(routed, 1)
            n_items = sp.value_load(items[0:1, 16:17], min_val=E, max_val=MAX_ITEMS)
            with sp.Fori(0, n_items) as n:
                e = sp.value_load(items[0:1, bass.ds(n, 1)], min_val=0, max_val=E - 1)
                for j in range(AHEAD, N_ITEM):
                    load(e, j, n * N_ITEM + (C_MOE + j))
                e = sp.value_load(items[0:1, bass.ds(n + 1, 1)], min_val=0, max_val=E - 1)
                for j in range(AHEAD):
                    load(e, j, n * N_ITEM + (C_MOE + N_ITEM + j))
            for i in range(RAW):
                n_pre = len([c for c in range(C_MOE) if c % RAW == i])
                sp.wait_ge(raw_full[i], n_items * (16 * N_ITEM // RAW) + 16 * (n_pre + 1))
                sp.sem_inc(sp_pace, 1)
            sp.wait_ge(turn_free, n_items * TURN_ITEM + (TURN0 + 4))
            sp.dma_start(out[0].rearrange("(t p) d -> p t d", p=P), h[:, :, :]).then_inc(stored, 16)
            sp.wait_ge(stored, 16)

        @block.gpsimd
        def _(pool):
            own = [0]

            def then(ins):
                own[0] += 1
                ins.then_inc(pool_own, 1)
                pool.wait_ge(pool_own, own[0])

            pool.wait_ge(turn_free, 2 + 4)
            keep = xs[:, :, :].rearrange("p t d -> p (t d)")
            then(nc.gpsimd.memset(keep, 1.0))
            nc.gpsimd.memset(keep.rearrange("p (c s) -> p c s", s=CH)[:, :, 0:1], 0.0).then_inc(keep_ready, 1)
            pool.wait_ge(proj_free, N_IN)
            for t in range(TT):
                g = og[:, t, :].rearrange("p (h e) -> p h e", e=HD)
                nc.gpsimd.tensor_tensor(g, g, gnorm[:, :].unsqueeze(1).to_broadcast([P, HEADS, HD]), MUL).then_inc(og_ready, 1)
            pool.wait_ge(att_split, KVH)
            nc.gpsimd.memset(gatT[:, :], 0.0)
            nc.gpsimd.memset(yb[:, :], 0.0).then_inc(yb_ready, 1)

            iota = const[:, K_IOTA:K_IOTA + P]

            def select(step):
                for t in range(TT):
                    for i in range(2):
                        step(nc.gpsimd.tensor_scalar(sel1[:, t, i, :], iota, pos[:, t, i:i + 1], 1.0, ALU.is_equal, MUL))
                        step(nc.gpsimd.tensor_scalar(gat1[:, t, i, :], sel1[:, t, i, :], gate[:, t, i:i + 1], 1.0, MUL, MUL))
                    step(nc.gpsimd.tensor_tensor(gat[:, t, :], gat1[:, t, 0, :], gat1[:, t, 1, :], ADD))
                    step(nc.gpsimd.tensor_tensor(sel[:, t, :], sel1[:, t, 0, :], sel1[:, t, 1, :], ADD))
                return nc.gpsimd.tensor_scalar(pos[:, :, :], pos[:, :, :], float(P), 1.0, SUB, MUL)

            pool.wait_ge(routed, 1)
            n_items = pool.value_load(items[0:1, 16:17], min_val=E, max_val=MAX_ITEMS)
            select(then).then_inc(sel_ready, 1)
            base = own[0]
            with pool.Fori(0, n_items) as n:
                pool.wait_ge(turned, n * TURN_ITEM + (TURN0 + GAT_TURN + 1))
                pool.sem_inc(pool_pace, 1)
                pool.wait_ge(sel_ready, n + 1)
                pool.sem_inc(pool_pace, 1)
                count = [0]

                def then_in_loop(ins):
                    count[0] += 1
                    ins.then_inc(pool_own, 1)
                    pool.wait_ge(pool_own, n * (2 * TT * 2 + 2 * TT) + (base + count[0]))
                    pool.sem_inc(pool_pace, 1)

                select(then_in_loop).then_inc(sel_ready, 1)
                assert count[0] == 2 * TT * 2 + 2 * TT

        @block.scalar
        def _(act):
            own = [0]
            nxt = [0]
            ta = [2]

            def then(ins):
                own[0] += 1
                ins.then_inc(act_own, 1)
                act.wait_ge(act_own, own[0])

            def round_chunk(c, slot_raw, raw_count, slot):
                act.wait_ge(raw_full[slot_raw], raw_count)
                if not (isinstance(c, int) and c < SPLIT):
                    act.wait_ge(chunk_used, c - (SPLIT - 1))
                nc.scalar.activation(w_hi[:, slot, :], raw[:, slot_raw, :], ACT.Copy).then_inc(hi_ready, 1)

            def round_to(c_last):
                while nxt[0] <= c_last:
                    c = nxt[0]
                    round_chunk(c, c % RAW, 16 * (c // RAW + 1), c % SPLIT)
                    nxt[0] += 1

            def inverse_root(n, width, wait_sem, wait_n):
                if wait_sem is not None:
                    act.wait_ge(wait_sem, wait_n)
                then(nc.scalar.activation(rstd[:, 0:n], ssq[:, 0:n], ACT.Ln, bias=eps[:, :], scale=1.0 / width))
                nc.scalar.activation(rstd[:, 0:n], rstd[:, 0:n], ACT.Exp, scale=-0.5).then_inc(rstd_ready, 1)

            def norm_stats():
                for t in range(TT):
                    then(nc.scalar.activation(xs[:, t, :], h[:, t, :], ACT.Square, accum_out=ssq[:, t:t + 1]))
                inverse_root(TT, D, None, 0)

            def turn_split(hi, gain_at):
                for u in range(4):
                    act.wait_ge(turned, ta[0] + 1)
                    bank = turn[ta[0] % 2]
                    if gain_at is None:
                        nc.scalar.activation(hi[:, 2 * u:2 * u + 2, :], bank[:, :].rearrange("p (k t) -> p k t", k=2),
                                             ACT.Copy).then_inc(turn_hi, 1)
                    else:
                        for k in range(2):
                            kt = 2 * u + k
                            ins = nc.scalar.activation(hi[:, kt, :], bank[:, 256 * k:256 * k + 256], ACT.Copy,
                                                       scale=cols[:, gain_at + kt:gain_at + kt + 1])
                        ins.then_inc(turn_hi, 1)
                    ta[0] += 1

            act.dma_start(h[:, :, :], a["x"][0].rearrange("(t p) d -> p t d", p=P)).then_inc(x_loaded, 16)
            loads = [
                (const[:, :], a["shape_constants"]),
                (vecs[0:16, :], a["attn_norm"].rearrange("l (r c) -> (l r) c", c=P)),
                (vecs[16:32, :], a["ffn_norm"].rearrange("l (r c) -> (l r) c", c=P)),
                (vecs[32:40, :], a["kv_norm"].rearrange("(r c) -> r c", c=P)),
                (vecs[40:64, :], a["hgrn_lb"].rearrange("l (r c) -> (l r) c", c=P)),
                (rel[:, :], a["rel_bias"]),
                (gain_row[:, :], a["ffn_norm"][1:2, :].to_broadcast([P, D])),
                (gnorm[:, :], a["hgrn_gnorm"][0:1, :].to_broadcast([P, HD])),
                (qgain[:, :], a["swa_q_gain"][0:1, :].to_broadcast([P, AD])),
                (kgain[:, :], a["k_gain"].unsqueeze(0).to_broadcast([P, AD])),
                (sink[:, :], a["swa_sink"][0:1, :].to_broadcast([P, QH])),
                (router[:, :, :], a["moe_router"][0].rearrange("(k p) e -> p k e", p=P)),
            ]
            assert len(loads) == 12
            for dst, src in loads:
                act.dma_start(dst, src).then_inc(params_loaded, 16)

            act.wait_ge(x_loaded, 16)
            act.wait_ge(eps_ready, 1)
            norm_stats()
            act.wait_ge(lb_logit, 1)
            nc.scalar.activation(lb[:, 0:3, :], lb[:, 0:3, :], ACT.Exp).then_inc(lb_exp, 1)
            act.wait_ge(bias_made, 1)
            act.dma_start(scratch, bias_row[:, :]).then_inc(bias_stored, 16)
            round_to(LEAD - 1)
            turn_split(ht_hi, 0)

            flatT = lambda buf: buf[:, :, :].rearrange("p h t -> p (h t)")
            for c in range(N_IN):
                round_to(c + LEAD)
                act.wait_ge(chunk_used, c + 1)
                bank = banks[c % 4]
                part, i = divmod(c, 4)
                if part == 0:
                    nc.scalar.activation(fT[:, 2 * i:2 * i + 2, :].rearrange("p h t -> p (h t)"), bank[:, :],
                                         ACT.Sigmoid).then_inc(proj_free, 1)
                elif part == 1:
                    nc.scalar.activation(qT[:, 2 * i:2 * i + 2, :].rearrange("p h t -> p (h t)"), bank[:, :],
                                         ACT.Copy).then_inc(proj_free, 1)
                else:
                    dst = val if part == 2 else og
                    nc.scalar.activation(dst[:, :, 256 * i:256 * i + 256], bank[:, :].rearrange("p (t c) -> p t c", t=2),
                                         ACT.Copy if part == 2 else ACT.Silu).then_inc(proj_free, 1)
                if c == 4:
                    act.wait_ge(f_ready, HEADS)
                    nc.scalar.activation(flatT(gT), flatT(fT), ACT.Ln).then_inc(ln_ready, 1)
                if c == 8:
                    act.wait_ge(rel_ready, 1)
                    nc.scalar.activation(flatT(eT), flatT(gT), ACT.Exp).then_inc(exp_ready, 1)
                if c == 10:
                    act.wait_ge(q_scaled, 1)
                    nc.scalar.activation(flatT(eT), flatT(gT), ACT.Exp, scale=-1.0).then_inc(expk_ready, 1)
                    act.wait_ge(decays, 1)
                    nc.scalar.activation(dec[:, :, :], dec[:, :, :], ACT.Exp).then_inc(dec_ready, 1)
            round_to(C_OUT + LEAD - 1)
            act.wait_ge(o_done, HEADS)
            for b in range(4):
                nc.scalar.activation(fT[:, 2 * b:2 * b + 2, :].rearrange("p h t -> p (h t)"), banks[b][:, :],
                                     ACT.Square).then_inc(sq_ready, 1)
            inverse_root(TT * HEADS, HD, ssq_ready, 1)
            turn_split(ht_hi, None)
            round_to(C_OUT + N_OUT - 1 + LEAD)

            act.wait_ge(h_ready, 1)
            norm_stats()
            turn_split(ht_hi, 16)
            for b in range(FF // 256):
                g = C_FF + 2 * b
                round_to(g + LEAD)
                act.wait_ge(chunk_used, g + 1)
                if b >= 2:
                    act.wait_ge(hid_ready, b - 1)
                nc.scalar.activation(ff_silu[:, b % 2, :], banks[2 * (b % 2)][:, :], ACT.Silu).then_inc(silu_ready, 1)
                round_to(g + 1 + LEAD)
                act.wait_ge(hid_ready, b + 1)
                nc.scalar.activation(mid_hi[:, 2 * b:2 * b + 2, :], ff_hid[:, b % 2, :].rearrange("p (k t) -> p k t", k=2),
                                     ACT.Copy).then_inc(mid_rounded, 1)
            round_to(C_KV - 1 + LEAD)

            act.wait_ge(h_ready, 2)
            act.wait_ge(bias_stored, 16)
            first = scratch[0:1, 0:1]
            rows = bass.AP(tensor=scratch.tensor, offset=first.offset, ap=[[1, P], [3 * P, QH], [1, 2 * P]])
            act.dma_start(bias_rev[:, :, :], rows).then_inc(bias_loaded, 16)
            norm_stats()
            for u in range(4):
                act.wait_ge(turned, ta[0] + 1)
                bank = turn[ta[0] % 2]
                for hi, at in ((kv_hi, 32), (ht_hi, 8)):
                    for k in range(2):
                        kt = 2 * u + k
                        ins = nc.scalar.activation(hi[:, kt, :], bank[:, 256 * k:256 * k + 256], ACT.Copy,
                                                   scale=cols[:, at + kt:at + kt + 1])
                ins.then_inc(turn_hi, 1)
                ta[0] += 1
            round_to(C_Q - 1 + LEAD)
            act.wait_ge(chunk_used, C_Q)
            for t in range(TT):
                nc.scalar.activation(vt[:, t, :], banks[t][:, 256:512], ACT.Copy).then_inc(kv_out, 1)
                nc.scalar.activation(kk[:, t, :], banks[t][:, 0:256], ACT.Copy).then_inc(kv_out, 1)
                nc.scalar.activation(ksq[:, t, :], banks[t][:, 0:256], ACT.Square).then_inc(kv_out, 1)
            inverse_root(TT * KVH, AD, ssq_ready, 2)
            ta[0] += TT
            round_to(C_O - 1 + LEAD)
            act.wait_ge(chunk_used, C_O)
            for t in range(TT):
                for half in range(2):
                    nc.scalar.activation(xs[:, t, 512 * half:512 * half + 512], banks[2 + 2 * t + half][:, :],
                                         ACT.Square).then_inc(sq_ready, 1)
            inverse_root(TT * QH, AD, ssq_ready, 3)
            ta[0] += 4

            def att_round(g):
                act.wait_ge(att_full, g + 1)
                nc.scalar.activation(ht_hi[:, 2 * g:2 * g + 2, :],
                                     banks[3 * (g % 2)][:, :].rearrange("p (k t) -> p k t", k=2), ACT.Copy).then_inc(att_hi, 1)

            for g in range(KVH):
                act.wait_ge(negm_ready, g + 1)
                if g >= 1:
                    act.wait_ge(turned, ta[0])
                l = banks[3 * (g % 2):3 * (g % 2) + 3]
                for hh in range(GRP):
                    nc.scalar.activation(pr[:, hh, :], l[0][:, P * hh:P * hh + P], ACT.Exp, bias=negm[:, g, 0, hh:hh + 1],
                                         accum_out=rsum[:, g, 0, hh:hh + 1])
                for hh in range(GRP):
                    ins = nc.scalar.activation(pr[:, 4 + 2 * hh:6 + 2 * hh, :].rearrange("p k c -> p (k c)"),
                                               l[1 + hh // 2][:, 256 * (hh % 2):256 * (hh % 2) + 256], ACT.Exp,
                                               bias=negm[:, g, 1, hh:hh + 1], accum_out=rsum[:, g, 1, hh:hh + 1])
                nc.scalar.activation(sinkd[:, g, :, :], sinkd[:, g, :, :], ACT.Exp).then_inc(exps_ready, 1)
                ta[0] += 3
                if g >= 1:
                    att_round(g - 1)
            att_round(KVH - 1)
            round_to(C_MOE - 1 + LEAD)

            act.wait_ge(h_ready, 3)
            norm_stats()
            for t in range(TT):
                act.wait_ge(hn_ready, t + 1)
                nc.scalar.activation(hn_hi[:, t, :], xs[:, t, :], ACT.Copy).then_inc(hn_rounded, 1)
            ta[0] += 4
            act.wait_ge(gap_ready, 1)
            nc.scalar.activation(gate[:, :, 1:2], gate[:, :, 1:2], ACT.Exp).then_inc(gap_exp, 1)

            def gather_round(k, u):
                act.wait_ge(turned, k + 1)
                nc.scalar.activation(ht_hi[:, 4 * u:4 * u + 4, 0:P], turn[u % 2][:, :].rearrange("p (k t) -> p k t", k=4),
                                     ACT.Copy).then_inc(turn_hi, 1)

            for u in range(2):
                gather_round(ta[0], u)
                ta[0] += 1
            assert ta[0] == TURN0 and TURN0 % 2 == 0 and nxt[0] == C_MOE + LEAD

            act.wait_ge(routed, 1)
            n_items = act.value_load(items[0:1, 16:17], min_val=E, max_val=MAX_ITEMS)
            with act.Fori(0, n_items) as n:
                for j in range(N_ITEM):
                    c0 = C_MOE + j + LEAD
                    round_chunk(n * N_ITEM + c0, c0 % RAW, n * (16 * N_ITEM // RAW) + 16 * (c0 // RAW + 1), c0 % SPLIT)
                    b, i = divmod(j, 4)
                    if b < BLK and i == 1:
                        act.wait_ge(chunk_used, n * N_ITEM + (C_MOE + j + 1))
                        act.wait_ge(hid_ready, n * BLK + (FF // 256 + max(b - 1, 0)))
                        nc.scalar.activation(e_silu[:, b % 2, :], banks[2 * (b % 2)][:, :], ACT.Silu).then_inc(silu_ready, 1)
                    hb = {4 * q + 5: q for q in range(BLK - 1)}.get(j, BLK - 1 if j == N_UP + 2 else None)
                    if hb is not None:
                        act.wait_ge(turned, n * TURN_ITEM + (TURN0 + HID_TURN[hb] + 1))
                        nc.scalar.activation(hid_hi[:, 4 * hb:4 * hb + 4, :],
                                             turn[HID_TURN[hb] % 2][:, :].rearrange("p (k t) -> p k t", k=4),
                                             ACT.Copy).then_inc(turn_hi, 1)
                    if j in (N_UP + 5, N_UP + 6):
                        u = j - N_UP - 5
                        gather_round(n * TURN_ITEM + (TURN0 + GATHER_TURN + u), u)
                act.wait_ge(chunk_used, n * N_ITEM + (C_MOE + N_ITEM))
                nc.scalar.activation(yb[:, 0:512], banks[4][:, :], ACT.Copy)
                nc.scalar.activation(yb[:, 512:1024], banks[5][:, :], ACT.Copy).then_inc(yb_ready, 1)

        @block.vector
        def _(dve):
            own = [0]
            nxt = [0]
            td = [0]

            def then(ins):
                own[0] += 1
                ins.then_inc(dve_own, 1)
                dve.wait_ge(dve_own, own[0])

            def rest_chunk(c, slot_raw, slot):
                dve.wait_ge(hi_ready, c + 1)
                nc.vector.tensor_tensor(w_lo[:, slot, :], raw[:, slot_raw, :], plain(w_hi[:, slot, :]), SUB).then_inc(split_ready, 1)

            def rest_to(c_last):
                while nxt[0] <= c_last:
                    c = nxt[0]
                    rest_chunk(c, c % RAW, c % SPLIT)
                    nxt[0] += 1

            def norm_rows(i):
                dve.wait_ge(rstd_ready, i)
                for t in range(TT):
                    nc.vector.tensor_scalar(xs[:, t, :], h[:, t, :], rstd[:, t:t + 1], None, MUL).then_inc(xs_ready, 1)

            def turn_rest(hi, lo, gain_at):
                for u in range(4):
                    dve.wait_ge(turn_hi, rounded[0] + 1)
                    bank = turn[td[0] % 2]
                    if gain_at is None:
                        nc.vector.tensor_tensor(lo[:, 2 * u:2 * u + 2, :], bank[:, :].rearrange("p (k t) -> p k t", k=2),
                                                plain(hi[:, 2 * u:2 * u + 2, :]), SUB).then_inc(turn_free, 1)
                    else:
                        for k in range(2):
                            kt = 2 * u + k
                            ins = nc.vector.scalar_tensor_tensor(
                                out=lo[:, kt, :], in0=bank[:, 256 * k:256 * k + 256],
                                scalar=cols[:, gain_at + kt:gain_at + kt + 1], in1=plain(hi[:, kt, :]), op0=MUL, op1=SUB)
                        ins.then_inc(turn_free, 1)
                    td[0] += 1
                    rounded[0] += 1

            def turn_copy(dst, part=None):
                dve.wait_ge(turned, td[0] + 1)
                src = turn[td[0] % 2][:, :] if part is None else turn[td[0] % 2][:, 0:part]
                if len(dst.shape) == 3:
                    src = src.rearrange("p (a b) -> p a b", a=dst.shape[1])
                nc.vector.tensor_copy(dst, src).then_inc(turn_free, 1)
                td[0] += 1

            def add_residual(bank_list):
                for t in range(TT):
                    for half in range(2):
                        part = h[:, t, 512 * half:512 * half + 512]
                        ins = nc.vector.tensor_tensor(part, part, bank_list[2 * t + half][:, :], ADD)
                ins.then_inc(h_ready, 1)

            rounded = [0]
            nc.vector.memset(eps[:, :], EPS).then_inc(eps_ready, 1)
            dve.wait_ge(params_loaded, 16 * 12)
            turn_copy(cols[:, :], 64)
            dve.wait_ge(turn_free, 1)
            l = [cols[:, 40 + 8 * i:48 + 8 * i] for i in range(3)]
            then(nc.vector.tensor_tensor(lb[:, 3, :], l[0], l[1], ALU.max))
            then(nc.vector.tensor_tensor(lb[:, 3, :], lb[:, 3, :], l[2], ALU.max))
            nc.vector.tensor_tensor(lb[:, 0:3, :], cols[:, 40:64].rearrange("p (l k) -> p l k", l=3),
                                    lb[:, 3:4, :].to_broadcast([P, 3, 8]), SUB).then_inc(lb_logit, 1)
            dve.wait_ge(turned, 2)
            nc.vector.tensor_tensor(bias_row[:, :], turn[1][0:QH, 0:3 * P], const[0:QH, K_MASK:K_MASK + 3 * P],
                                    ADD).then_inc(bias_made, 1)
            dve.wait_ge(bias_made, 1)
            nc.vector.tensor_scalar(qgain[:, :], qgain[:, :], AD ** -0.5, None, MUL).then_inc(turn_free, 1)
            td[0] += 1
            norm_rows(1)
            dve.wait_ge(lb_exp, 1)
            then(nc.vector.tensor_tensor(lb[:, 4, :], lb[:, 0, :], lb[:, 1, :], ADD))
            then(nc.vector.tensor_tensor(lb[:, 4, :], lb[:, 4, :], lb[:, 2, :], ADD))
            then(nc.vector.reciprocal(lb[:, 5, :], lb[:, 4, :]))
            then(nc.vector.tensor_tensor(lb[:, 6, :], lb[:, 0, :], lb[:, 5, :], MUL))
            then(nc.vector.tensor_scalar(lb[:, 7, :], lb[:, 6, :], -1.0, 1.0, MUL, ADD))
            rest_to(LEAD - 1)
            turn_rest(ht_hi, ht_lo, 0)

            def chunks(buf):
                return buf[:, :, :].rearrange("p h (c s) -> p h c s", s=CH)

            flatT = lambda buf: buf[:, :, :].rearrange("p h t -> p (h t)")
            for c in range(N_IN):
                rest_to(c + LEAD)
                if c < 4:
                    dve.wait_ge(proj_free, c + 1)
                    for hd in (2 * c, 2 * c + 1):
                        nc.vector.tensor_scalar(fT[:, hd, :], fT[:, hd, :], lb[:, 7, hd:hd + 1], lb[:, 6, hd:hd + 1],
                                                MUL, ADD).then_inc(f_ready, 1)
                if c == 5:
                    dve.wait_ge(ln_ready, 1)
                    nc.vector.tensor_scalar(flatT(fT), flatT(fT), -1.0, 1.0, MUL, ADD)
                    dve.wait_ge(keep_ready, 1)
                    then(nc.vector.tensor_tensor_scan(flatT(eT), xs[:, :, :].rearrange("p t d -> p (t d)"), flatT(gT),
                                                      0.0, MUL, ADD))
                if c == 6:
                    then(nc.vector.tensor_copy(mid[:, :, :], chunks(eT)[:, :, :, CH // 2 - 1]))
                    then(nc.vector.tensor_copy(tot[:, :, :], chunks(eT)[:, :, :, CH - 1]))
                    nc.vector.tensor_tensor(chunks(gT), chunks(eT), mid[:, :, :].unsqueeze(3).to_broadcast([P, HEADS, NCH, CH]),
                                            SUB).then_inc(rel_ready, 1)
                    dve.wait_ge(rel_ready, 1)
                    for i in range(1, NCH):
                        if i > 1:
                            then(nc.vector.tensor_tensor(tot[:, :, i - 1], tot[:, :, i - 1], tot[:, :, i - 2], ADD))
                        then(nc.vector.tensor_tensor(mid[:, :, i], mid[:, :, i], tot[:, :, i - 1], ADD))
                    k = 0
                    for j in range(NCH - 1):
                        for i in range(j + 1, NCH):
                            ins = nc.vector.tensor_tensor(dec[:, k, :], mid[:, :, i], mid[:, :, j], SUB)
                            k += 1
                    ins.then_inc(decays, 1)
                if c == 9:
                    dve.wait_ge(exp_ready, 1)
                    dve.wait_ge(proj_free, 8)
                    nc.vector.tensor_tensor(flatT(qT), flatT(qT), flatT(eT), MUL).then_inc(q_scaled, 1)
                if c == 11:
                    dve.wait_ge(expk_ready, 1)
                    nc.vector.tensor_tensor(flatT(fT), flatT(fT), flatT(eT), MUL)
                    dve.wait_ge(dec_ready, 1)
                    dve.wait_ge(q_scaled, 1)
                if c in (11, 12, 13):
                    j = c - 11
                    k = sum(NCH - 1 - jj for jj in range(j))
                    for i in range(j + 1, NCH):
                        ins = nc.vector.tensor_tensor(q_from[j][:, :, i - j - 1, :], chunks(qT)[:, :, i, :],
                                                      dec[:, k + i - j - 1, :].unsqueeze(2).to_broadcast([P, HEADS, CH]), MUL)
                    if c == 13:
                        ins.then_inc(hgrn_ready, 1)
            rest_to(C_OUT + LEAD - 1)
            for hd in range(HEADS):
                dve.wait_ge(sc_full, hd + 1)
                if hd >= 2:
                    dve.wait_ge(o_done, hd - 1)
                nc.vector.tensor_tensor(sc[:, hd % 2, :], banks[4 + hd % 2][:, 0:3 * P], const[:, K_TRI:K_TRI + 3 * P],
                                        MUL).then_inc(sc_masked, 1)
            dve.wait_ge(sq_ready, 4)
            nc.vector.tensor_reduce(ssq[:, 0:TT * HEADS], fT[:, :, :].rearrange("p h t -> p (h t)").rearrange("p (n e) -> p n e", e=HD),
                                    AX.X, ADD).then_inc(ssq_ready, 1)
            dve.wait_ge(rstd_ready, 2)
            dve.wait_ge(og_ready, TT)
            y = flatT(qT)
            for b in range(4):
                nc.vector.tensor_tensor(y[:, 512 * b:512 * b + 512].rearrange("p (h e) -> p h e", e=HD),
                                        banks[b][:, :].rearrange("p (h e) -> p h e", e=HD),
                                        rstd[:, 4 * b:4 * b + 4].unsqueeze(2).to_broadcast([P, 4, HD]), MUL).then_inc(dve_own, 1)
                own[0] += 1
            dve.wait_ge(dve_own, own[0])
            for t in range(TT):
                nc.vector.tensor_tensor(y[:, D * t:D * t + D], y[:, D * t:D * t + D], og[:, t, :], MUL).then_inc(xs_ready, 1)
            turn_rest(ht_hi, ht_lo, None)
            rest_to(C_OUT + N_OUT - 1 + LEAD)
            dve.wait_ge(chunk_used, C_FF)
            add_residual(banks[0:4])

            norm_rows(3)
            turn_rest(ht_hi, ht_lo, 16)
            for b in range(FF // 256):
                g = C_FF + 2 * b
                rest_to(g + 1 + LEAD)
                if b >= 1:
                    dve.wait_ge(mid_rounded, b)
                    nc.vector.tensor_tensor(mid_lo[:, 2 * b - 2:2 * b, :], ff_hid[:, (b - 1) % 2, :].rearrange("p (k t) -> p k t", k=2),
                                            plain(mid_hi[:, 2 * b - 2:2 * b, :]), SUB).then_inc(mid_split, 1)
                dve.wait_ge(silu_ready, b + 1)
                dve.wait_ge(chunk_used, g + 2)
                nc.vector.tensor_tensor(ff_hid[:, b % 2, :], ff_silu[:, b % 2, :], banks[2 * (b % 2) + 1][:, :],
                                        MUL).then_inc(hid_ready, 1)
            b = FF // 256
            dve.wait_ge(mid_rounded, b)
            nc.vector.tensor_tensor(mid_lo[:, 2 * b - 2:2 * b, :], ff_hid[:, (b - 1) % 2, :].rearrange("p (k t) -> p k t", k=2),
                                    plain(mid_hi[:, 2 * b - 2:2 * b, :]), SUB).then_inc(mid_split, 1)
            rest_to(C_KV - 1 + LEAD)
            dve.wait_ge(chunk_used, C_KV)
            add_residual([banks[4], banks[5], banks[2], banks[3]])

            norm_rows(4)
            then(nc.vector.memset(kT[:, :, :, :], 0.0))
            for u in range(4):
                dve.wait_ge(turn_hi, rounded[0] + 1)
                bank = turn[td[0] % 2]
                for hi, lo, at in ((kv_hi, kv_lo, 32), (ht_hi, ht_lo, 8)):
                    for k in range(2):
                        kt = 2 * u + k
                        ins = nc.vector.scalar_tensor_tensor(
                            out=lo[:, kt, :], in0=bank[:, 256 * k:256 * k + 256], scalar=cols[:, at + kt:at + kt + 1],
                            in1=plain(hi[:, kt, :]), op0=MUL, op1=SUB)
                ins.then_inc(turn_free, 1)
                td[0] += 1
                rounded[0] += 1
            rest_to(C_Q - 1 + LEAD)
            dve.wait_ge(kv_out, 3 * TT)
            heads = lambda ap: ap.rearrange("p (n e) -> p n e", e=AD)
            kflat = kk[:, :, :].rearrange("p t c -> p (t c)")
            nc.vector.tensor_reduce(ssq[:, 0:TT * KVH], heads(ksq[:, :, :].rearrange("p t c -> p (t c)")), AX.X, ADD).then_inc(ssq_ready, 1)
            dve.wait_ge(rstd_ready, 5)
            then(nc.vector.tensor_tensor(heads(kflat), heads(kflat), rstd[:, 0:TT * KVH].unsqueeze(2).to_broadcast([P, TT * KVH, AD]), MUL))
            for i in range(2):
                nc.vector.tensor_tensor(k2[:, :, :, i, :].rearrange("p t g e -> p (t g) e"), heads(kflat),
                                        kgain[:, :].unsqueeze(1).to_broadcast([P, TT * KVH, AD]), MUL).then_inc(xs_ready, 1)
            rest_to(C_O - 1 + LEAD)
            for t in range(TT):
                dve.wait_ge(turned, td[0] + 1)
                for i in range(2):
                    rows = slice(AD * i, AD * i + AD)
                    ins = nc.vector.tensor_copy(kT[rows, i, :, P * t:P * t + P],
                                                turn[td[0] % 2][rows, :].rearrange("p (g c) -> p g c", g=KVH))
                ins.then_inc(turn_free, 1)
                td[0] += 1
            dve.wait_ge(sq_ready, 4 + 4)
            nc.vector.tensor_reduce(ssq[:, 0:TT * QH], heads(xs[:, :, :].rearrange("p t c -> p (t c)")), AX.X, ADD).then_inc(ssq_ready, 1)
            dve.wait_ge(rstd_ready, 6)
            for t in range(TT):
                for half in range(2):
                    n0 = QH * t + 8 * half
                    then(nc.vector.tensor_tensor(heads(xs[:, t, 512 * half:512 * half + 512]), heads(banks[2 + 2 * t + half][:, :]),
                                                 rstd[:, n0:n0 + 8].unsqueeze(2).to_broadcast([P, 8, AD]), MUL))
                nc.vector.tensor_tensor(heads(xs[:, t, :]), heads(xs[:, t, :]),
                                        qgain[:, :].unsqueeze(1).to_broadcast([P, QH, AD]), MUL).then_inc(xs_ready, 1)
            for t in range(TT):
                for u in range(2):
                    turn_copy(aqT[:, 4 * u:4 * u + 4, P * t:P * t + P])

            def largest(g):
                dve.wait_ge(logits_full, g + 1)
                l = banks[3 * (g % 2):3 * (g % 2) + 3]
                then(nc.vector.reduce_max(mx[:, g, 0, :], l[0][:, :].rearrange("p (h k) -> p h k", h=4), axis=AX.X))
                for i in range(2):
                    then(nc.vector.reduce_max(mx[:, g, 1, 2 * i:2 * i + 2], l[1 + i][:, :].rearrange("p (h k) -> p h k", h=2), axis=AX.X))
                snk = sink[:, GRP * g:GRP * g + GRP].unsqueeze(1).to_broadcast([P, TT, GRP])
                then(nc.vector.tensor_tensor(mx[:, g, :, :], mx[:, g, :, :], snk, ALU.max))
                then(nc.vector.tensor_tensor(sinkd[:, g, :, :], snk, mx[:, g, :, :], SUB))
                nc.vector.tensor_scalar(negm[:, g, :, :], mx[:, g, :, :], -1.0, None, MUL).then_inc(negm_ready, 1)

            def normalise(g):
                dve.wait_ge(exps_ready, g + 1)
                then(nc.vector.tensor_tensor(rsum[:, g, :, :], rsum[:, g, :, :], sinkd[:, g, :, :], ADD))
                then(nc.vector.reciprocal(rsum[:, g, :, :], rsum[:, g, :, :]))
                nc.vector.tensor_tensor(pr[:, 0:4, :], pr[:, 0:4, :], rsum[:, g, 0, :].unsqueeze(2).to_broadcast([P, 4, P]),
                                        MUL).then_inc(probs_ready, 1)
                p1 = pr[:, 4:12, :].rearrange("p (h k) c -> p h (k c)", k=2)
                nc.vector.tensor_tensor(p1, p1, rsum[:, g, 1, :].unsqueeze(2).to_broadcast([P, 4, 2 * P]), MUL).then_inc(probs_ready, 1)

            def att_rest(g):
                dve.wait_ge(att_hi, g + 1)
                nc.vector.tensor_tensor(ht_lo[:, 2 * g:2 * g + 2, :], banks[3 * (g % 2)][:, :].rearrange("p (k t) -> p k t", k=2),
                                        plain(ht_hi[:, 2 * g:2 * g + 2, :]), SUB).then_inc(att_split, 1)

            largest(0)
            for g in range(KVH):
                normalise(g)
                if g >= 1:
                    dve.wait_ge(att_full, g)
                    att_rest(g - 1)
                for u in range(3):
                    turn_copy(pT[:, 4 * u:4 * u + 4, :])
                if g + 1 < KVH:
                    largest(g + 1)
            att_rest(KVH - 1)
            rest_to(C_MOE - 1 + LEAD)
            dve.wait_ge(chunk_used, C_MOE)
            add_residual([banks[1], banks[2], banks[4], banks[5]])

            norm_rows(7)
            dve.wait_ge(xs_ready, 14)
            for t in range(TT):
                nc.vector.tensor_tensor(xs[:, t, :], xs[:, t, :], gain_row[:, :], MUL).then_inc(hn_ready, 1)
            for t in range(TT):
                dve.wait_ge(hn_rounded, t + 1)
                nc.vector.tensor_tensor(hn_lo[:, t, :], xs[:, t, :], plain(hn_hi[:, t, :]), SUB).then_inc(hn_split, 1)
            for u in range(4):
                turn_copy(hnT[:, 2 * u:2 * u + 2, :])
            dve.wait_ge(logit_full, 1)
            iota8 = const[:, K_IOTA:K_IOTA + E]
            then(nc.vector.tensor_copy(lg[:, :, :], banks[0][:, 0:TT * E].rearrange("p (t e) -> p t e", e=E)))
            for t in range(TT):
                then(nc.vector.max(out=top[:, t, :], in_=lg[:, t, :]))
                then(nc.vector.max_index(out=topi[:, t, :], in_max=top[:, t, :], in_values=lg[:, t, :]))
                then(nc.vector.tensor_copy(topf[:, t, :], topi[:, t, 0:2]))
                for i in range(2):
                    then(nc.vector.tensor_scalar(hot[:, t, i, :], iota8, topf[:, t, i:i + 1], None, ALU.is_equal))
            nc.vector.tensor_tensor(mask[:, :, :], hot[:, :, 0, :], hot[:, :, 1, :], ADD).then_inc(mask_ready, 1)
            nc.vector.tensor_tensor(gate[:, :, 1:2], top[:, :, 1:2], top[:, :, 0:1], SUB).then_inc(gap_ready, 1)
            dve.wait_ge(rank_full, 1)
            then(nc.vector.tensor_copy(rank[:, :, :], banks[1][:, 0:3 * E].rearrange("p (t e) -> p t e", e=E)))
            over, which, ones, base, shift = (r1[:, i, :] for i in range(5))
            then(nc.vector.tensor_scalar(over, rank[:, 2, :], float(P), None, ALU.is_gt))
            then(nc.vector.memset(ones, 1.0))
            then(nc.vector.tensor_tensor_scan(which, ones, over, 0.0, MUL, ADD))
            then(nc.vector.tensor_scalar(itf[0:1, 16:17], which[0:1, E - 1:E], float(E), None, ADD))
            then(nc.vector.tensor_tensor(which, which, over, SUB))
            then(nc.vector.tensor_scalar(base, iota8, float(P), None, MUL))
            then(nc.vector.tensor_tensor(shift, which, iota8, SUB))
            then(nc.vector.tensor_scalar(shift, shift, float(P), float(P * (E - 1)), MUL, ADD))
            for t in range(TT):
                big = r1[:, 5, :]
                then(nc.vector.tensor_scalar(big, rank[:, t, :], float(P), None, ALU.is_ge))
                then(nc.vector.tensor_tensor(big, big, shift, MUL))
                then(nc.vector.tensor_tensor(big, big, base, ADD))
                then(nc.vector.tensor_tensor(rank[:, t, :], rank[:, t, :], big, ADD))
                for i in range(2):
                    then(nc.vector.tensor_tensor(hot[:, t, i, :], hot[:, t, i, :], rank[:, t, :], MUL))
            then(nc.vector.tensor_reduce(pos[:, :, :].rearrange("p t i -> p (t i)"), hot[:, :, :, :].rearrange("p t i e -> p (t i) e"), AX.X, ADD))
            dve.wait_ge(gap_exp, 1)
            then(nc.vector.tensor_scalar(gate[:, :, 0:1], gate[:, :, 1:2], 1.0, None, ADD))
            then(nc.vector.reciprocal(gate[:, :, 0:1], gate[:, :, 0:1]))
            then(nc.vector.tensor_tensor(gate[:, :, 1:2], gate[:, :, 1:2], gate[:, :, 0:1], MUL))
            row8 = const[0:1, K_IOTA:K_IOTA + 8]
            along = lambda v: v.unsqueeze(1).to_broadcast([1, 8, E])
            then(nc.vector.tensor_tensor(it[:, 0, :, :], along(r1[0:1, 1, :]), row8.unsqueeze(2).to_broadcast([1, 8, E]), ALU.is_equal))
            then(nc.vector.tensor_tensor(r1[0:1, 6, :], r1[0:1, 0, :], row8, MUL))
            then(nc.vector.tensor_tensor(it[:, 1, :, :], it[:, 0, :, :], along(r1[0:1, 6, :]), MUL))
            then(nc.vector.tensor_reduce(itf[0:1, 8:16], it[:, 1, :, :], AX.X, ADD))
            then(nc.vector.tensor_copy(itf[0:1, 0:8], row8))
            nc.vector.tensor_copy(items[0:1, 0:17], itf[0:1, 0:17]).then_inc(routed, 1)

            def gather_rest(k_hi, u):
                dve.wait_ge(turn_hi, k_hi + 1)
                nc.vector.tensor_tensor(ht_lo[:, 4 * u:4 * u + 4, 0:P], turn[u % 2][:, :].rearrange("p (k t) -> p k t", k=4),
                                        plain(ht_hi[:, 4 * u:4 * u + 4, 0:P]), SUB).then_inc(turn_free, 1)

            for u in range(2):
                gather_rest(rounded[0], u)
                rounded[0] += 1
                td[0] += 1
            assert td[0] == TURN0 and nxt[0] == C_MOE + LEAD
            r0 = rounded[0]

            def scatter_add(k, s):
                t, half = divmod(s, 2)
                part = h[:, t, 512 * half:512 * half + 512]
                dve.wait_ge(turned, k + 1)
                return nc.vector.tensor_tensor(part, part, turn[s % 2][:, :], ADD)

            dve.wait_ge(routed, 1)
            n_items = dve.value_load(items[0:1, 16:17], min_val=E, max_val=MAX_ITEMS)
            with dve.Fori(0, n_items) as n:
                for j in range(N_ITEM):
                    c0 = C_MOE + j + LEAD
                    rest_chunk(n * N_ITEM + c0, c0 % RAW, c0 % SPLIT)
                    b, i = divmod(j, 4)
                    if b < BLK and i == 3:
                        dve.wait_ge(silu_ready, n * BLK + (FF // 256 + b + 1))
                        dve.wait_ge(chunk_used, n * N_ITEM + (C_MOE + j + 1))
                        nc.vector.tensor_tensor(e_hid[:, b % 2, :], e_silu[:, b % 2, :], banks[2 * (b % 2) + 1][:, :],
                                                MUL).then_inc(hid_ready, 1)
                    if 2 <= j < 6:
                        scatter_add(n * TURN_ITEM + (TURN0 + j - 2), j - 2).then_inc(turn_free, 1)
                    if j == 10:
                        dve.wait_ge(turned, n * TURN_ITEM + (TURN0 + GAT_TURN + 1))
                        nc.vector.tensor_copy(gatT[:, :], turn[GAT_TURN % 2][:, 0:T]).then_inc(turn_free, 1)
                    hb = {4 * q + 5: q for q in range(BLK - 1)}.get(j, BLK - 1 if j == N_UP + 2 else None)
                    if hb is not None:
                        dve.wait_ge(turn_hi, n * (BLK + 2) + (r0 + hb + 1))
                        nc.vector.tensor_tensor(hid_lo[:, 4 * hb:4 * hb + 4, :],
                                                turn[HID_TURN[hb] % 2][:, :].rearrange("p (k t) -> p k t", k=4),
                                                plain(hid_hi[:, 4 * hb:4 * hb + 4, :]), SUB).then_inc(turn_free, 1)
                    if j in (N_UP + 5, N_UP + 6):
                        u = j - N_UP - 5
                        gather_rest(n * (BLK + 2) + (r0 + BLK + u), u)
            for s in range(4):
                scatter_add(n_items * TURN_ITEM + (TURN0 + s), s).then_inc(turn_free, 1)

        @block.tensor
        def _(pe):
            tp = [0]
            ident = const[:, K_ID:K_ID + P]

            def product(dst, st, mv, first, last):
                nc.tensor.matmul(dst, st[0], mv[0], start=first, stop=False)
                nc.tensor.matmul(dst, st[0], mv[1], start=False, stop=False)
                return nc.tensor.matmul(dst, st[1], mv[0], start=False, stop=last)

            def turn_bank():
                if tp[0] >= 2:
                    pe.wait_ge(turn_free, tp[0] - 1)
                bank = turn[tp[0] % 2]
                tp[0] += 1
                return bank

            def turn_rows(rows):
                for u in range(4):
                    bank = turn_bank()
                    for k in range(2):
                        for t in range(TT):
                            kt = 2 * u + k
                            ins = nc.tensor.transpose(bank[:, 256 * k + P * t:256 * k + P * t + P],
                                                      rows(t)[:, P * kt:P * kt + P], ident)
                    ins.then_inc(turned, 1)

            def to_features(c, bank, hi, lo):
                pe.wait_ge(split_ready, c + 1)
                wh, wl = split_view(w_hi, c, 256), split_view(w_lo, c, 256)
                for half in range(2):
                    for k in range(KT):
                        cut = slice(P * half, P * half + P)
                        ins = product(bank[:, 256 * half:256 * half + 256], (wh[:, k, cut], wl[:, k, cut]),
                                      (hi[:, k, :], lo[:, k, :]), k == 0, k == KT - 1)
                ins.then_inc(chunk_used, 1)

            def to_rows(c, width, kts, k0, n_k, hi, lo, dst):
                pe.wait_ge(split_ready, c + 1)
                wh, wl = split_view(w_hi, c, width), split_view(w_lo, c, width)
                for t in range(TT):
                    for q in range(max(1, width // 512)):
                        w = min(width, 512)
                        for k in range(kts):
                            kt = k0 + k
                            tok = slice(P * t, P * t + P)
                            cut = slice(w * q, w * q + w)
                            ins = product(dst(t, q), (hi[:, kt, tok], lo[:, kt, tok]), (wh[:, k, cut], wl[:, k, cut]),
                                          kt == 0, kt == n_k - 1)
                ins.then_inc(chunk_used, 1)

            pe.wait_ge(params_loaded, 16 * 12)
            nc.tensor.transpose(turn_bank()[:, 0:64], vecs[:, :], const[0:64, K_ID:K_ID + 64]).then_inc(turned, 1)
            nc.tensor.matmul(turn_bank()[0:QH, 0:3 * P], rel[:, :], const[0:BUCKETS, K_HOT:K_HOT + 3 * P],
                             start=True, stop=True).then_inc(turned, 1)
            pe.wait_ge(xs_ready, TT)
            turn_rows(lambda t: xs[:, t, :])
            pe.wait_ge(turn_free, tp[0])

            for c in range(N_IN):
                if c >= 4:
                    pe.wait_ge(proj_free, c - 3)
                if c < 8:
                    to_features(c, banks[c % 4], ht_hi, ht_lo)
                else:
                    to_rows(c, 256, KT, 0, KT, ht_hi, ht_lo, lambda t, q, bank=banks[c % 4]: bank[:, 256 * t:256 * t + 256])
            pe.wait_ge(proj_free, N_IN)
            pe.wait_ge(hgrn_ready, 1)

            def scores(hd):
                if hd >= 2:
                    pe.wait_ge(sc_masked, hd - 1)
                bank = banks[4 + hd % 2]
                key = lambda j: fT[:, hd, CH * j:CH * j + CH]
                whole = lambda bank_rows, at, w, st, mv: nc.tensor.matmul(bank[bank_rows:bank_rows + CH, at:at + w], st, mv, start=True, stop=True)
                later = lambda j, i, n: q_from[j][:, hd, i - j - 1:i - j - 1 + n, :].rearrange("p i s -> p (i s)")
                whole(0, 0, CH, key(0), qT[:, hd, 0:CH])
                whole(0, CH, CH, key(0), later(0, 1, 1))
                whole(0, 2 * P, P, key(0), later(0, 2, 2))
                whole(CH, 0, P, key(1), qT[:, hd, 0:P])
                whole(CH, 2 * P, P, key(1), later(1, 2, 2))
                whole(0, P, CH, key(2), qT[:, hd, P:P + CH])
                whole(0, P + CH, CH, key(2), later(2, 3, 1))
                whole(CH, P, P, key(3), qT[:, hd, P:T]).then_inc(sc_full, 1)

            def readout(hd):
                pe.wait_ge(sc_masked, hd + 1)
                at = HD * (hd % 4)
                d0 = banks[hd // 4][:, at:at + HD]
                d1 = banks[2 + hd // 4][:, at:at + HD]
                s_ = sc[:, hd % 2, :]
                v0, v1 = (val[:, t, HD * hd:HD * hd + HD] for t in range(2))
                nc.tensor.matmul(d0, s_[:, 0:P], v0, start=True, stop=True)
                nc.tensor.matmul(d1, s_[:, 2 * P:3 * P], v0, start=True, stop=False)
                nc.tensor.matmul(d1, s_[:, P:2 * P], v1, start=False, stop=True).then_inc(o_done, 1)

            scores(0)
            for hd in range(HEADS):
                if hd + 1 < HEADS:
                    scores(hd + 1)
                readout(hd)
            pe.wait_ge(xs_ready, 2 * TT)
            turn_rows(lambda t: qT[:, :, :].rearrange("p h t -> p (h t)")[:, D * t:D * t + D])
            pe.wait_ge(turn_free, tp[0])
            for i in range(N_OUT):
                to_rows(C_OUT + i, D, 2, 2 * i, KT, ht_hi, ht_lo, lambda t, q: banks[2 * t + q][:, :])

            pe.wait_ge(xs_ready, 3 * TT)
            turn_rows(lambda t: xs[:, t, :])
            pe.wait_ge(turn_free, tp[0])
            for b in range(FF // 256):
                if b >= 2:
                    pe.wait_ge(hid_ready, b - 1)
                for i in range(2):
                    to_features(C_FF + 2 * b + i, banks[2 * (b % 2) + i], ht_hi, ht_lo)
            down_bank = [[banks[4], banks[5]], [banks[2], banks[3]]]
            for i in range(N_DOWN):
                pe.wait_ge(mid_split, i + 1)
                to_rows(C_DOWN + i, D, 2, 2 * i, FF // P, mid_hi, mid_lo, lambda t, q: down_bank[t][q][:, :])

            pe.wait_ge(xs_ready, 4 * TT)
            turn_rows(lambda t: xs[:, t, :])
            pe.wait_ge(turn_free, tp[0])
            for i in range(N_KV):
                to_rows(C_KV + i, 512, 4, 4 * i, KT, kv_hi, kv_lo, lambda t, q: banks[t][:, :])
            for i in range(N_Q):
                to_rows(C_Q + i, D, 2, 2 * i, KT, ht_hi, ht_lo, lambda t, q: banks[2 + 2 * t + q][:, :])
            pe.wait_ge(xs_ready, 4 * TT + 2)
            for t in range(TT):
                bank = turn_bank()
                for g in range(KVH):
                    ins = nc.tensor.transpose(bank[:, P * g:P * g + P], k2[:, t, g, :, :].rearrange("p i e -> p (i e)"), ident)
                ins.then_inc(turned, 1)
            for t in range(TT):
                pe.wait_ge(xs_ready, 4 * TT + 2 + t + 1)
                for u in range(2):
                    bank = turn_bank()
                    for k in range(4):
                        ins = nc.tensor.transpose(bank[:, P * k:P * k + P], xs[:, t, P * (4 * u + k):P * (4 * u + k) + P], ident)
                    ins.then_inc(turned, 1)
            pe.wait_ge(turn_free, tp[0])
            pe.wait_ge(bias_loaded, 16)

            def logits(g):
                if g >= 2:
                    pe.wait_ge(att_split, g - 1)
                l = banks[3 * (g % 2):3 * (g % 2) + 3]
                anti = const[:, K_ANTI:K_ANTI + P]
                for t in range(TT):
                    for hh in range(GRP):
                        head = GRP * g + hh
                        q = aqT[:, head // 2, P * t:P * t + P]
                        if t == 0:
                            dst, keys, bias = l[0][:, P * hh:P * hh + P], slice(0, P), slice(P, 2 * P)
                        else:
                            dst, keys, bias = l[1 + hh // 2][:, 256 * (hh % 2):256 * (hh % 2) + 256], slice(0, T), slice(0, 2 * P)
                        nc.tensor.matmul(dst, anti, bias_rev[:, head, bias], start=True, stop=False)
                        ins = nc.tensor.matmul(dst, q, kT[:, hh % 2, g, keys], start=False, stop=True)
                ins.then_inc(logits_full, 1)

            def attend(g):
                for u in range(3):
                    bank = turn_bank()
                    pe.wait_ge(probs_ready, 2 * g + (1 if u == 0 else 2))
                    for k in range(4):
                        ins = nc.tensor.transpose(bank[:, P * k:P * k + P], pr[:, 4 * u + k, :], ident)
                    ins.then_inc(turned, 1)
                pe.wait_ge(turn_free, tp[0])
                bank = banks[3 * (g % 2)]
                for hh in range(GRP):
                    row, at = AD * (hh % 2), 256 * (hh // 2)
                    v = [vt[:, t, AD * g:AD * g + AD] for t in range(TT)]
                    d = bank[row:row + AD, at:at + 2 * P]
                    nc.tensor.matmul(d[:, 0:P], v[0], pT[:, hh, :], start=True, stop=True)
                    nc.tensor.matmul(d[:, P:2 * P], v[0], pT[:, 4 + 2 * hh, :], start=True, stop=False)
                    ins = nc.tensor.matmul(d[:, P:2 * P], v[1], pT[:, 5 + 2 * hh, :], start=False, stop=True)
                ins.then_inc(att_full, 1)

            logits(0)
            logits(1)
            for g in range(KVH):
                attend(g)
                if g + 2 < KVH:
                    logits(g + 2)
            pe.wait_ge(att_split, KVH)
            o_bank = [[banks[1], banks[2]], [banks[4], banks[5]]]
            for i in range(N_O):
                to_rows(C_O + i, D, 2, 2 * i, KT, ht_hi, ht_lo, lambda t, q: o_bank[t][q][:, :])

            pe.wait_ge(hn_ready, TT)
            turn_rows(lambda t: xs[:, t, :])
            pe.wait_ge(turn_free, tp[0])
            for t in range(TT):
                for k in range(KT):
                    ins = nc.tensor.matmul(banks[0][:, E * t:E * t + E], hnT[:, k, P * t:P * t + P], router[:, k, :],
                                           start=k == 0, stop=k == KT - 1)
            ins.then_inc(logit_full, 1)
            pe.wait_ge(mask_ready, 1)
            before, every = const[:, K_STRICT:K_STRICT + P], const[:, K_TRI + 2 * P:K_TRI + 3 * P]
            m = [mask[:, t, :] for t in range(TT)]
            r = [banks[1][:, E * i:E * i + E] for i in range(3)]
            nc.tensor.matmul(r[0], before, m[0], start=True, stop=True)
            nc.tensor.matmul(r[1], every, m[0], start=True, stop=False)
            nc.tensor.matmul(r[1], before, m[1], start=False, stop=True)
            nc.tensor.matmul(r[2], every, m[0], start=True, stop=False)
            nc.tensor.matmul(r[2], every, m[1], start=False, stop=True).then_inc(rank_full, 1)

            def gather(u):
                for k in range(4):
                    kt = 4 * u + k
                    for t in range(TT):
                        for i, part in enumerate((hn_hi, hn_lo)):
                            ins = nc.tensor.matmul(turn[u % 2][:, P * k:P * k + P], part[:, t, P * kt:P * kt + P], sel[:, t, :],
                                                   start=t + i == 0, stop=t + i == 2)
                ins.then_inc(turned, 1)

            def scatter(s):
                t, half = divmod(s, 2)
                nc.tensor.matmul(turn[s % 2][:, :], gatT[:, P * t:P * t + P], yb[:, 512 * half:512 * half + 512],
                                 start=True, stop=True).then_inc(turned, 1)

            pe.wait_ge(hn_split, TT)
            pe.wait_ge(sel_ready, 1)
            for u in range(2):
                turn_bank()
                gather(u)
            assert tp[0] == TURN0

            pe.wait_ge(routed, 1)
            n_items = pe.value_load(items[0:1, 16:17], min_val=E, max_val=MAX_ITEMS)
            with pe.Fori(0, n_items) as n:
                def free_turn(i):
                    pe.wait_ge(turn_free, n * TURN_ITEM + (TURN0 + i - 1))

                for j in range(N_ITEM):
                    c0 = C_MOE + j
                    b, i = divmod(j, 4)
                    if j == 0:
                        pe.wait_ge(turn_free, n * TURN_ITEM + TURN0)
                    if j < N_UP and i == 0:
                        pe.wait_ge(hid_ready, n * BLK + (FF // 256 + max(b - 1, 0)))
                    if j >= N_UP:
                        d = j - N_UP
                        if d % 2 == 0:
                            pe.wait_ge(turn_free, n * TURN_ITEM + (TURN0 + HID_TURN[d // 2] + 1))
                    pe.wait_ge(split_ready, n * N_ITEM + (c0 + 1))
                    if j < N_UP:
                        wh, wl = split_view(w_hi, c0, 512), split_view(w_lo, c0, 512)
                        bank = banks[2 * (b % 2) + i // 2]
                        for k in range(4):
                            kt = 4 * (i % 2) + k
                            ins = product(bank[:, :], (ht_hi[:, kt, 0:P], ht_lo[:, kt, 0:P]), (wh[:, k, :], wl[:, k, :]),
                                          kt == 0, kt == KT - 1)
                    else:
                        wh, wl = split_view(w_hi, c0, D), split_view(w_lo, c0, D)
                        for k in range(2):
                            kt = 2 * d + k
                            for q in range(2):
                                cut = slice(512 * q, 512 * q + 512)
                                ins = product(banks[4 + q][:, :], (hid_hi[:, kt, :], hid_lo[:, kt, :]),
                                              (wh[:, k, cut], wl[:, k, cut]), kt == 0, kt == FKT - 1)
                    ins.then_inc(chunk_used, 1)
                    if 2 <= j < 6:
                        s_ = j - 2
                        if s_ == 0:
                            pe.wait_ge(yb_ready, n + 1)
                        free_turn(s_)
                        scatter(s_)
                    if j == 10:
                        pe.wait_ge(sel_ready, n + 1)
                        free_turn(GAT_TURN)
                        for t in range(TT):
                            ins = nc.tensor.transpose(turn[GAT_TURN % 2][:, P * t:P * t + P], gat[:, t, :], ident)
                        ins.then_inc(turned, 1)
                    hb = {4 * q + 5: q for q in range(BLK - 1)}.get(j, BLK - 1 if j == N_UP + 2 else None)
                    if hb is not None:
                        pe.wait_ge(hid_ready, n * BLK + (FF // 256 + hb + 1))
                        free_turn(HID_TURN[hb])
                        for k in range(4):
                            ins = nc.tensor.transpose(turn[HID_TURN[hb] % 2][:, P * k:P * k + P],
                                                      e_hid[:, hb % 2, P * k:P * k + P], ident)
                        ins.then_inc(turned, 1)
                    if j in (N_UP + 5, N_UP + 6):
                        u = j - N_UP - 5
                        pe.wait_ge(sel_ready, n + 2)
                        free_turn(GATHER_TURN + u)
                        gather(u)
            for s_ in range(4):
                pe.wait_ge(turn_free, n_items * TURN_ITEM + (TURN0 + s_ - 1))
                if s_ == 0:
                    pe.wait_ge(yb_ready, n_items + 1)
                scatter(s_)


_INS = ["x", "hgrn_w_in", "hgrn_lb", "hgrn_gnorm", "hgrn_w_out", "swa_w_q", "swa_q_gain", "swa_sink", "swa_w_o",
        "kv_norm", "kv_w", "k_gain", "rel_bias", "attn_norm", "ffn_norm", "ffn_w_gate", "ffn_w_up", "ffn_w_down",
        "moe_router", "moe_w_gate", "moe_w_up", "moe_w_down"]


def kernel(**inputs):
    import concourse.bacc as bacc
    from concourse.bass_utils import run_bass_kernel_spmd

    nc = bacc.Bacc("TRN2", target_bir_lowering=False, num_devices=1)
    arrays = {name: np.ascontiguousarray(inputs[name]) for name in _INS}
    arrays["shape_constants"] = shape_constants()
    aps = {name: nc.dram_tensor(f"in_{name}", v.shape, mybir.dt.from_np(v.dtype), kind="ExternalInput").ap()
           for name, v in arrays.items()}
    out = nc.dram_tensor("out", (1, T, D), mybir.dt.float32, kind="ExternalOutput").ap()
    build_program(nc, aps, out)
    r = run_bass_kernel_spmd(nc, [{f"in_{k}": v for k, v in arrays.items()}], core_ids=[0])
    return r.results[0]["out"]
```

```python
import math
from contextlib import ExitStack

import numpy as np
import concourse.bass as bass
from concourse import mybir

P = 128
D = 1024
KT = D // P
T = 256
TT = T // P
HEADS, HD = 8, 128
CH = 64
NCH = T // CH
QH, KVH, AD = 16, 4, 64
GRP = QH // KVH
WIN = 128
BUCKETS, MAX_DIST = 32, 128
FF = 2816
E, FE = 8, 3584
FKT = FE // P
EPS = 1e-6
MASKED = -1e30

CW = 2048
RAW, SPLIT = 6, 3
LEAD = 2
N_IN, N_OUT, N_FF, N_DOWN, N_KV, N_Q, N_O = 16, 4, 2 * FF // 256, FF // 256, 2, 4, 4
C_OUT = N_IN
C_FF = C_OUT + N_OUT
C_DOWN = C_FF + N_FF
C_KV = C_DOWN + N_DOWN
C_Q = C_KV + N_KV
C_O = C_Q + N_Q
C_MOE = C_O + N_O
BLK = FE // 512
N_UP = 4 * BLK
N_ITEM = N_UP + FKT // 2
ITEM_LEAD = SPLIT
AHEAD = RAW + ITEM_LEAD
MAX_ITEMS = 11

K_ID, K_ANTI, K_TRI, K_STRICT, K_IOTA, K_HOT, K_MASK, K_END = 0, 128, 256, 640, 768, 896, 1280, 1664


def shape_constants():
    c = np.zeros((P, K_END), np.float32)
    r = np.arange(P)
    c[:, K_ID:K_ID + P] = r[:, None] == r[None]
    c[:, K_ANTI:K_ANTI + P] = r[:, None] + r[None] == P - 1
    upper = r[:, None] <= r[None]
    c[:, K_TRI:K_TRI + P] = upper
    c[:, K_TRI + P:K_TRI + 2 * P] = upper
    c[:, K_TRI + 2 * P:K_TRI + 3 * P] = 1.0
    c[:, K_STRICT:K_STRICT + P] = r[:, None] < r[None]
    c[:, K_IOTA:K_IOTA + P] = r[None]
    exact = BUCKETS // 2
    for m in range(3 * P):
        dist = 2 * P - 1 - m
        if 0 <= dist < WIN:
            b = dist
            if dist >= exact:
                f = np.log(np.float32(dist) / np.float32(exact)) / np.float32(math.log(MAX_DIST / exact))
                b = min(exact + int(np.float32(f) * np.float32(BUCKETS - exact)), BUCKETS - 1)
            c[b, K_HOT + m] = 1.0
        else:
            c[:, K_MASK + m] = MASKED
    return c


def build_program(nc, a, out):
    f32, f32r = mybir.dt.float32, mybir.dt.float32r
    i32, u32 = mybir.dt.int32, mybir.dt.uint32
    ALU, ACT, AX = mybir.AluOpType, mybir.ActivationFunctionType, mybir.AxisListType
    MUL, ADD, SUB = ALU.mult, ALU.add, ALU.subtract

    def plain(ap):
        return ap.bitcast(f32)

    w_in = a["hgrn_w_in"][0]
    deep = lambda w, c, n: w[:, c:c + n].rearrange("(k p) c -> p k c", p=P)
    flat = lambda w, r, n: w[r:r + n, :].rearrange("(k p) c -> p k c", p=P)
    stream = []
    for part in (1, 0, 2, 3):
        stream += [deep(w_in, part * D + 256 * i, 256) for i in range(4)]
    stream += [flat(a["hgrn_w_out"][0], 256 * i, 256) for i in range(N_OUT)]
    for b in range(FF // 256):
        stream += [deep(a["ffn_w_gate"][0], 256 * b, 256), deep(a["ffn_w_up"][0], 256 * b, 256)]
    stream += [flat(a["ffn_w_down"][0], 256 * i, 256) for i in range(N_DOWN)]
    stream += [flat(a["kv_w"], 512 * i, 512) for i in range(N_KV)]
    stream += [flat(a["swa_w_q"][0], 256 * i, 256) for i in range(N_Q)]
    stream += [flat(a["swa_w_o"][0], 256 * i, 256) for i in range(N_O)]
    assert len(stream) == C_MOE and C_MOE % SPLIT == 0 and N_ITEM % RAW == 0 and N_ITEM % SPLIT == 0

    def item_source(e, j):
        if j < N_UP:
            b, i = divmod(j, 4)
            w = a["moe_w_gate"] if i < 2 else a["moe_w_up"]
            r = 512 * (i % 2)
            return w[0][bass.ds(e, 1), r:r + 512, 512 * b:512 * b + 512].rearrange("e (k p) c -> p (e k) c", p=P)
        r = 256 * (j - N_UP)
        return a["moe_w_down"][0][bass.ds(e, 1), r:r + 256, :].rearrange("e (k p) c -> p (e k) c", p=P)

    scratch = nc.dram_tensor("bias_rows", [QH, 3 * P], f32, kind="Internal").ap()

    ctx = ExitStack()
    with ctx:
        def sb(stack, name, shape, dt=f32):
            return stack.enter_context(nc.sbuf_tensor(name, shape, dt))

        def sem(name):
            return ctx.enter_context(nc.semaphore(name))

        raw = sb(ctx, "raw", [P, RAW, CW])
        w_hi = sb(ctx, "w_hi", [P, SPLIT, CW], f32r)
        w_lo = sb(ctx, "w_lo", [P, SPLIT, CW], f32r)
        h = sb(ctx, "h", [P, TT, D])
        ht_hi = sb(ctx, "ht_hi", [P, KT, T], f32r)
        ht_lo = sb(ctx, "ht_lo", [P, KT, T], f32r)
        xs = sb(ctx, "xs", [P, TT, D])
        const = sb(ctx, "const", [P, K_END])
        vecs = sb(ctx, "vecs", [64, P])
        cols = sb(ctx, "cols", [P, 64])
        gain_row = sb(ctx, "gain_row", [P, D])
        gnorm = sb(ctx, "gnorm", [P, HD])
        qgain = sb(ctx, "qgain", [P, AD])
        kgain = sb(ctx, "kgain", [P, AD])
        sink = sb(ctx, "sink", [P, QH])
        rel = sb(ctx, "rel", [BUCKETS, QH])
        router = sb(ctx, "router", [P, KT, E])
        bias_row = sb(ctx, "bias_row", [QH, 3 * P])
        eps = sb(ctx, "eps", [P, 1])
        warm = sb(ctx, "warm", [P, 1])
        minus_half = sb(ctx, "minus_half", [P, TT])
        ssq = sb(ctx, "ssq", [P, 32])
        rstd = sb(ctx, "rstd", [P, 32])
        lb = sb(ctx, "lb", [P, 8, 8])
        items = sb(ctx, "items", [1, 32], i32)

        s = ExitStack()
        fT = sb(s, "fT", [P, HEADS, T])
        qT = sb(s, "qT", [P, HEADS, T])
        gT = sb(s, "gT", [P, HEADS, T])
        eT = sb(s, "eT", [P, HEADS, T])
        q_from = [sb(s, f"q_from{j}", [P, HEADS, NCH - 1 - j, CH]) for j in range(NCH - 1)]
        val = sb(s, "val", [P, TT, D])
        og = sb(s, "og", [P, TT, D])
        sc = sb(s, "sc", [P, 2, 3 * P])
        mid = sb(s, "mid", [P, HEADS, NCH])
        tot = sb(s, "tot", [P, HEADS, NCH])
        dec = sb(s, "dec", [P, 6, HEADS])
        s.close()
        s = ExitStack()
        mid_hi = sb(s, "mid_hi", [P, FF // P, T], f32r)
        mid_lo = sb(s, "mid_lo", [P, FF // P, T], f32r)
        ff_silu = sb(s, "ff_silu", [P, 2, 512])
        ff_hid = sb(s, "ff_hid", [P, 2, 512])
        s.close()
        s = ExitStack()
        bias_rev = sb(s, "bias_rev", [P, QH, 2 * P])
        vt = sb(s, "vt", [P, TT, 256])
        kT = sb(s, "kT", [P, 2, KVH, T])
        aqT = sb(s, "aqT", [P, QH // 2, T])
        prs = [sb(s, "pr0", [P, 12, P])]
        pTs = [sb(s, "pT0", [P, 12, P])]
        kvs = ExitStack()
        kv_hi = sb(kvs, "kv_hi", [P, KT, T], f32r)
        kv_lo = sb(kvs, "kv_lo", [P, KT, T], f32r)
        kvs.close()
        pairs = ExitStack()
        prs.append(sb(pairs, "pr1", [P, 12, P]))
        pTs.append(sb(pairs, "pT1", [P, 12, P]))
        pairs.close()
        over_kv = sb(s, "over_kv", [P, 2 * KT * T])
        kk = pTs[0][:, 0:4, :].rearrange("p (t k) c -> p t (k c)", t=TT)
        ksq = prs[0][:, 0:4, :].rearrange("p (t k) c -> p t (k c)", t=TT)
        k2 = prs[0][:, 4:12, :].rearrange("p (t g) (i e) -> p t g i e", t=TT, i=2)
        mx = sb(s, "mx", [P, KVH, TT, GRP])
        negm = sb(s, "negm", [P, KVH, TT, GRP])
        sinkd = sb(s, "sinkd", [P, KVH, TT, GRP])
        rsum = sb(s, "rsum", [P, KVH, TT, GRP])
        s.close()
        s = ExitStack()
        hid_hi = sb(s, "hid_hi", [P, FKT, P], f32r)
        hid_lo = sb(s, "hid_lo", [P, FKT, P], f32r)
        hn_hi = sb(s, "hn_hi", [P, TT, D], f32r)
        hn_lo = sb(s, "hn_lo", [P, TT, D], f32r)
        sel = sb(s, "sel", [P, TT, P], f32r)
        sel1 = sb(s, "sel1", [P, TT, 2, P])
        gat1 = sb(s, "gat1", [P, TT, 2, P])
        gat = sb(s, "gat", [P, TT, P])
        gatT = sb(s, "gatT", [P, T])
        yb = sb(s, "yb", [P, D])
        pos = sb(s, "pos", [P, TT, 2])
        gate = sb(s, "gate", [P, TT, 2])
        rt = ExitStack()
        hnT = sb(rt, "hnT", [P, KT, T])
        rt.close()
        e_silu = sb(s, "e_silu", [P, 2, 512])
        e_hid = sb(s, "e_hid", [P, 2, 512])
        s.close()
        lg = sb(ctx, "lg", [P, TT, E])
        lgT = sb(ctx, "lgT", [E, T])
        top = sb(ctx, "top", [P, TT, 8])
        topi = sb(ctx, "topi", [P, TT, 8], u32)
        topf = sb(ctx, "topf", [P, TT, 2])
        hot = sb(ctx, "hot", [P, TT, 2, E])
        mask = sb(ctx, "mask", [P, TT, E])
        rank = sb(ctx, "rank", [P, TT, E])
        big = sb(ctx, "big", [P, TT, E])
        over = sb(ctx, "over", [P, E + 1])
        which = sb(ctx, "which", [P, E + 1])
        ones = sb(ctx, "ones", [P, E + 1])
        base = sb(ctx, "base", [P, E])
        late = sb(ctx, "late", [P, E])
        iota_p = sb(ctx, "iota_p", [1, E])
        it = sb(ctx, "it", [1, 2, 8, E])
        itf = sb(ctx, "itf", [1, 32])

        banks = [ctx.enter_context(nc.psum_tensor(f"bank{i}", [P, 512], f32)) for i in range(8)]
        turn = banks[6:8]

        raw_full = [sem(f"raw_full{i}") for i in range(RAW)]
        hi_ready = sem("hi_ready")
        split_ready = sem("split_ready")
        chunk_used = sem("chunk_used")
        tile_done = sem("tile_done")
        params_loaded = sem("params_loaded")
        consts_loaded = sem("consts_loaded")
        x_loaded = [sem(f"x_loaded{t}") for t in range(TT)]
        stats_ready = sem("stats_ready")
        act_own = sem("act_own")
        dve_own = sem("dve_own")
        pool_own = sem("pool_own")
        turned = sem("turned")
        turn_hi = sem("turn_hi")
        turn_free = sem("turn_free")
        eps_ready = sem("eps_ready")
        rstd_ready = sem("rstd_ready")
        root_ready = sem("root_ready")
        xs_ready = sem("xs_ready")
        bias_made = sem("bias_made")
        bias_stored = sem("bias_stored")
        bias_loaded = sem("bias_loaded")
        proj_free = sem("proj_free")
        f_ready = sem("f_ready")
        lb_logit = sem("lb_logit")
        lb_exp = sem("lb_exp")
        ln_ready = sem("ln_ready")
        rel_ready = sem("rel_ready")
        exp_ready = sem("exp_ready")
        q_scaled = sem("q_scaled")
        expk_ready = sem("expk_ready")
        dec_ready = sem("dec_ready")
        decays = sem("decays")
        hgrn_ready = sem("hgrn_ready")
        keep_ready = sem("keep_ready")
        og_ready = sem("og_ready")
        y_ready = sem("y_ready")
        o_done = sem("o_done")
        sq_ready = sem("sq_ready")
        ssq_ready = sem("ssq_ready")
        h_ready = sem("h_ready")
        keys_zeroed = sem("keys_zeroed")
        silu_ready = sem("silu_ready")
        hid_ready = sem("hid_ready")
        mid_rounded = sem("mid_rounded")
        mid_split = sem("mid_split")
        kv_out = sem("kv_out")
        logits_full = sem("logits_full")
        negm_ready = sem("negm_ready")
        exps_ready = sem("exps_ready")
        probs_ready = sem("probs_ready")
        hn_ready = sem("hn_ready")
        hn_rounded = sem("hn_rounded")
        hn_split = sem("hn_split")
        logit_full = sem("logit_full")
        lgT_ready = sem("lgT_ready")
        mask_ready = sem("mask_ready")
        rank_full = sem("rank_full")
        gap_ready = sem("gap_ready")
        gap_exp = sem("gap_exp")
        routed = sem("routed")
        yb_ready = sem("yb_ready")
        first_sel = sem("first_sel")
        sel_ready = sem("sel_ready")
        stored = sem("stored")
        sp_pace = sem("sp_pace")
        pool_pace = sem("pool_pace")

        block = ctx.enter_context(nc.Block())

        def proj_bank(c):
            return banks[c % 4] if c < 12 else banks[4 + c % 2]

        def split_view(buf, c, width):
            return buf[:, c % SPLIT, :].rearrange("p (k c) -> p k c", c=width)

        TURN_ITEM = 14
        HID_TURN = [4, 5, 7, 8, 9, 10, 11]
        GAT_TURN, GATHER_TURN = 6, 12
        TURN_ATT = 2 + 4 + HEADS + 4 + 4 + 4 + TT + 4 + 4 * KVH
        TURN0 = TURN_ATT + 4 + 2

        @block.sync
        def _(sp):
            for t in range(TT):
                sp.dma_start(h[:, t, :], a["x"][0][P * t:P * t + P, :]).then_inc(x_loaded[t], 16)
            for dst, src in ((const[:, 0:K_HOT], a["shape_constants"][:, 0:K_HOT]),
                             (vecs[0:16, :], a["attn_norm"].rearrange("l (r c) -> (l r) c", c=P)),
                             (vecs[16:32, :], a["ffn_norm"].rearrange("l (r c) -> (l r) c", c=P)),
                             (vecs[32:40, :], a["kv_norm"].rearrange("(r c) -> r c", c=P)),
                             (vecs[40:64, :], a["hgrn_lb"].rearrange("l (r c) -> (l r) c", c=P))):
                sp.dma_start(dst, src).then_inc(consts_loaded, 16)
            loads = [
                (const[:, K_HOT:K_END], a["shape_constants"][:, K_HOT:K_END]),
                (rel[:, :], a["rel_bias"]),
                (gain_row[:, :], a["ffn_norm"][1:2, :].to_broadcast([P, D])),
                (gnorm[:, :], a["hgrn_gnorm"][0:1, :].to_broadcast([P, HD])),
                (qgain[:, :], a["swa_q_gain"][0:1, :].to_broadcast([P, AD])),
                (kgain[:, :], a["k_gain"].unsqueeze(0).to_broadcast([P, AD])),
                (sink[:, :], a["swa_sink"][0:1, :].to_broadcast([P, QH])),
                (router[:, :, :], a["moe_router"][0].rearrange("(k p) e -> p k e", p=P)),
            ]
            for c, src in enumerate(stream):
                if c == 4:
                    for param, values in loads:
                        sp.dma_start(param, values).then_inc(params_loaded, 16)
                if c >= RAW:
                    sp.wait_ge(split_ready, c - RAW + 1)
                dst = raw[:, c % RAW, :].rearrange("p (k c) -> p k c", k=src.shape[1])
                sp.dma_start(dst, src).then_inc(raw_full[c % RAW], 16)

            def load(e, j, c):
                src = item_source(e, j)
                sp.wait_ge(split_ready, c - RAW + 1)
                if not isinstance(c, int):
                    sp.sem_inc(sp_pace, 1)
                slot = (C_MOE + j) % RAW
                dst = raw[:, slot, :].rearrange("p (k c) -> p k c", k=src.shape[1])
                sp.dma_start(dst, src).then_inc(raw_full[slot], 16)

            for j in range(AHEAD):
                load(0, j, C_MOE + j)
            sp.wait_ge(routed, 1)
            n_items = sp.value_load(items[0:1, 16:17], min_val=E, max_val=MAX_ITEMS)
            with sp.Fori(1, n_items) as n:
                e = sp.value_load(items[0:1, bass.ds(n - 1, 1)], min_val=0, max_val=E - 1)
                for j in range(AHEAD, N_ITEM):
                    load(e, j, n * N_ITEM + (C_MOE - N_ITEM + j))
                e = sp.value_load(items[0:1, bass.ds(n, 1)], min_val=0, max_val=E - 1)
                for j in range(AHEAD):
                    load(e, j, n * N_ITEM + (C_MOE + j))
            e = sp.value_load(items[0:1, bass.ds(n_items - 1, 1)], min_val=0, max_val=E - 1)
            for j in range(AHEAD, N_ITEM):
                load(e, j, n_items * N_ITEM + (C_MOE - N_ITEM + j))
            for j in range(ITEM_LEAD):
                sp.wait_ge(split_ready, n_items * N_ITEM + (C_MOE + j - RAW + 1))
                sp.sem_inc(raw_full[(C_MOE + j) % RAW], 16)
            for i in range(RAW):
                n_pre = len([c for c in range(C_MOE + ITEM_LEAD) if c % RAW == i])
                sp.wait_ge(raw_full[i], n_items * (16 * N_ITEM // RAW) + 16 * n_pre)
                sp.sem_inc(sp_pace, 1)
            for t in range(TT):
                sp.wait_ge(turn_free, n_items * TURN_ITEM + (TURN0 + 2 * t + 2))
                sp.sem_inc(sp_pace, 1)
                sp.dma_start(out[0][P * t:P * t + P, :], h[:, t, :]).then_inc(stored, 16)
            sp.wait_ge(stored, 16 * TT)

        @block.gpsimd
        def _(pool):
            own = [0]

            def then(ins):
                own[0] += 1
                ins.then_inc(pool_own, 1)
                pool.wait_ge(pool_own, own[0])

            def inverse_root(i):
                pool.wait_ge(stats_ready, TT * i)
                if i > 1:
                    pool.wait_ge(h_ready, TT * (i - 1))
                then(nc.gpsimd.tensor_scalar(rstd[:, 0:TT], ssq[:, 0:TT], 1.0 / D, EPS, MUL, ADD))
                nc.gpsimd.tensor_tensor(rstd[:, 0:TT], rstd[:, 0:TT], minus_half[:, :], ALU.pow).then_inc(rstd_ready, 1)

            then(nc.gpsimd.memset(minus_half[:, :], -0.5))
            inverse_root(1)
            pool.wait_ge(turn_free, 1 + 4)
            keep = xs[:, :, :].rearrange("p t d -> p (t d)")
            then(nc.gpsimd.memset(keep, 1.0))
            nc.gpsimd.memset(keep.rearrange("p (c s) -> p c s", s=CH)[:, :, 0:1], 0.0).then_inc(keep_ready, 1)
            pool.wait_ge(proj_free, N_IN)
            for t in range(TT):
                g = og[:, t, :].rearrange("p (h e) -> p h e", e=HD)
                nc.gpsimd.tensor_tensor(g, g, gnorm[:, :].unsqueeze(1).to_broadcast([P, HEADS, HD]), MUL).then_inc(og_ready, 1)
            inverse_root(2)
            inverse_root(3)
            nc.gpsimd.memset(kT[:, :, :, :].rearrange("p i g t -> p (i g t)"), 0.0).then_inc(keys_zeroed, 1)
            pool.wait_ge(turn_free, TURN_ATT)
            nc.gpsimd.memset(gatT[:, :], 0.0)
            nc.gpsimd.memset(yb[:, :], 0.0).then_inc(yb_ready, 1)
            inverse_root(4)
            for t in range(TT):
                pool.wait_ge(hn_rounded, t + 1)
                nc.gpsimd.tensor_tensor(hn_lo[:, t, :], xs[:, t, :], plain(hn_hi[:, t, :]), SUB).then_inc(hn_split, 1)

            iota = const[:, K_IOTA:K_IOTA + P]

            def select(step, gathers):
                for t in range(TT):
                    for i in range(2):
                        step(nc.gpsimd.tensor_scalar(sel1[:, t, i, :], iota, pos[:, t, i:i + 1], 1.0, ALU.is_equal, MUL))
                        step(nc.gpsimd.tensor_scalar(gat1[:, t, i, :], sel1[:, t, i, :], gate[:, t, i:i + 1], 1.0, MUL, MUL))
                    step(nc.gpsimd.tensor_tensor(gat[:, t, :], gat1[:, t, 0, :], gat1[:, t, 1, :], ADD))
                    if gathers:
                        step(nc.gpsimd.tensor_tensor(sel[:, t, :], sel1[:, t, 0, :], sel1[:, t, 1, :], ADD))
                return nc.gpsimd.tensor_scalar(pos[:, :, :], pos[:, :, :], float(P), 1.0, SUB, MUL)

            pool.wait_ge(routed, 1)
            n_items = pool.value_load(items[0:1, 16:17], min_val=E, max_val=MAX_ITEMS)
            select(then, False).then_inc(sel_ready, 1)
            base = own[0]
            with pool.Fori(0, n_items) as n:
                pool.wait_ge(turned, n * TURN_ITEM + (TURN0 + GAT_TURN + 1))
                pool.sem_inc(pool_pace, 1)
                pool.wait_ge(sel_ready, n + 1)
                pool.sem_inc(pool_pace, 1)
                count = [0]

                def then_in_loop(ins):
                    count[0] += 1
                    ins.then_inc(pool_own, 1)
                    pool.wait_ge(pool_own, n * (2 * TT * 2 + 2 * TT) + (base + count[0]))
                    pool.sem_inc(pool_pace, 1)

                select(then_in_loop, True).then_inc(sel_ready, 1)
                assert count[0] == 2 * TT * 2 + 2 * TT

        @block.scalar
        def _(act):
            own = [0]
            nxt = [0]
            ta = [1]

            def then(ins):
                own[0] += 1
                ins.then_inc(act_own, 1)
                act.wait_ge(act_own, own[0])

            def round_chunk(c, slot_raw, raw_count, slot):
                act.wait_ge(raw_full[slot_raw], raw_count)
                if not (isinstance(c, int) and c < SPLIT):
                    act.wait_ge(chunk_used, c - (SPLIT - 1))
                nc.scalar.activation(w_hi[:, slot, :], raw[:, slot_raw, :], ACT.Copy).then_inc(hi_ready, 1)

            def round_to(c_last):
                while nxt[0] <= c_last:
                    c = nxt[0]
                    round_chunk(c, c % RAW, 16 * (c // RAW + 1), c % SPLIT)
                    nxt[0] += 1

            def head_roots(at, n, width, count):
                act.wait_ge(ssq_ready, count)
                nc.scalar.activation(rstd[:, at:at + n], ssq[:, at:at + n], ACT.Sqrt, bias=eps[:, :], scale=1.0 / width).then_inc(root_ready, 1)

            def norm_stats(i):
                for t in range(TT):
                    if i:
                        act.wait_ge(h_ready, TT * (i - 1) + t + 1)
                    else:
                        act.wait_ge(x_loaded[t], 16)
                    nc.scalar.activation(xs[:, t, :], h[:, t, :], ACT.Square, accum_out=ssq[:, t:t + 1]).then_inc(stats_ready, 1)

            def turn_split(hi, gain_at):
                for u in range(4):
                    act.wait_ge(turned, ta[0] + 1)
                    bank = turn[ta[0] % 2]
                    if gain_at is None:
                        nc.scalar.activation(hi[:, 2 * u:2 * u + 2, :], bank[:, :].rearrange("p (k t) -> p k t", k=2),
                                             ACT.Copy).then_inc(turn_hi, 1)
                    else:
                        for k in range(2):
                            kt = 2 * u + k
                            ins = nc.scalar.activation(hi[:, kt, :], bank[:, 256 * k:256 * k + 256], ACT.Copy,
                                                       scale=cols[:, gain_at + kt:gain_at + kt + 1])
                        ins.then_inc(turn_hi, 1)
                    ta[0] += 1

            act.wait_ge(eps_ready, 1)
            nc.scalar.activation(warm[:, :], eps[:, :], ACT.Square)
            norm_stats(0)
            act.wait_ge(lb_logit, 1)
            nc.scalar.activation(lb[:, 0:3, :], lb[:, 0:3, :], ACT.Exp).then_inc(lb_exp, 1)
            round_to(0)
            turn_split(ht_hi, 0)
            round_to(LEAD - 1)
            ta[0] += 1

            flatT = lambda buf: buf[:, :, :].rearrange("p h t -> p (h t)")
            for c in range(N_IN):
                round_to(c + LEAD)
                act.wait_ge(chunk_used, c + 1)
                if c == 3:
                    act.wait_ge(bias_made, 1)
                    act.dma_start(scratch, bias_row[:, :]).then_inc(bias_stored, 16)
                bank = proj_bank(c)
                part, i = divmod(c, 4)
                if part == 0:
                    nc.scalar.activation(fT[:, 2 * i:2 * i + 2, :].rearrange("p h t -> p (h t)"), bank[:, :],
                                         ACT.Sigmoid).then_inc(proj_free, 1)
                elif part == 1:
                    nc.scalar.activation(qT[:, 2 * i:2 * i + 2, :].rearrange("p h t -> p (h t)"), bank[:, :],
                                         ACT.Copy).then_inc(proj_free, 1)
                else:
                    dst = val if part == 2 else og
                    nc.scalar.activation(dst[:, :, 256 * i:256 * i + 256], bank[:, :].rearrange("p (t c) -> p t c", t=2),
                                         ACT.Copy if part == 2 else ACT.Silu).then_inc(proj_free, 1)
                if c == 4:
                    act.wait_ge(f_ready, HEADS)
                    nc.scalar.activation(flatT(gT), flatT(fT), ACT.Ln).then_inc(ln_ready, 1)
                if c == 8:
                    act.wait_ge(rel_ready, 1)
                    nc.scalar.activation(flatT(eT), flatT(gT), ACT.Exp).then_inc(exp_ready, 1)
                if c == 10:
                    act.wait_ge(q_scaled, 1)
                    nc.scalar.activation(flatT(eT), flatT(gT), ACT.Exp, scale=-1.0).then_inc(expk_ready, 1)
                    act.wait_ge(decays, 1)
                    nc.scalar.activation(dec[:, :, :], dec[:, :, :], ACT.Exp).then_inc(dec_ready, 1)
            nc.scalar.activation(warm[:, :], eps[:, :], ACT.Sqrt)
            for i in range(2):
                act.wait_ge(o_done, 4 * i + 4)
                for t in range(TT):
                    b = 2 * t + i
                    nc.scalar.activation(eT[:, 2 * b:2 * b + 2, :].rearrange("p h t -> p (h t)"), banks[b][:, :],
                                         ACT.Square).then_inc(sq_ready, 1)
                head_roots(4 * TT * i, 4 * TT, HD, TT * (i + 1))
            ta[0] += HEADS
            turn_split(ht_hi, None)
            round_to(C_OUT + N_OUT - 1 + LEAD)

            norm_stats(1)
            turn_split(ht_hi, 16)
            for b in range(FF // 256):
                g = C_FF + 2 * b
                round_to(g + LEAD)
                act.wait_ge(chunk_used, g + 1)
                if b >= 2:
                    act.wait_ge(hid_ready, b - 1)
                nc.scalar.activation(ff_silu[:, b % 2, :], banks[2 * (b % 2)][:, :], ACT.Silu).then_inc(silu_ready, 1)
                round_to(g + 1 + LEAD)
                act.wait_ge(hid_ready, b + 1)
                nc.scalar.activation(mid_hi[:, 2 * b:2 * b + 2, :], ff_hid[:, b % 2, :].rearrange("p (k t) -> p k t", k=2),
                                     ACT.Copy).then_inc(mid_rounded, 1)
            round_to(C_KV - 1 + LEAD)

            act.wait_ge(h_ready, 2 * TT)
            act.wait_ge(bias_stored, 16)
            first = scratch[0:1, 0:1]
            rows = bass.AP(tensor=scratch.tensor, offset=first.offset, ap=[[1, P], [3 * P, QH], [1, 2 * P]])
            norm_stats(2)
            act.dma_start(bias_rev[:, :, :], rows).then_inc(bias_loaded, 16)
            for u in range(4):
                act.wait_ge(turned, ta[0] + 1)
                bank = turn[ta[0] % 2]
                for hi, at in ((kv_hi, 32), (ht_hi, 8)):
                    for k in range(2):
                        kt = 2 * u + k
                        ins = nc.scalar.activation(hi[:, kt, :], bank[:, 256 * k:256 * k + 256], ACT.Copy,
                                                   scale=cols[:, at + kt:at + kt + 1])
                ins.then_inc(turn_hi, 1)
                ta[0] += 1
            round_to(C_Q - 1 + LEAD)
            act.wait_ge(chunk_used, C_Q)
            for t in range(TT):
                nc.scalar.activation(vt[:, t, :], banks[t][:, 256:512], ACT.Copy).then_inc(kv_out, 1)
                nc.scalar.activation(kk[:, t, :], banks[t][:, 0:256], ACT.Copy).then_inc(kv_out, 1)
                nc.scalar.activation(ksq[:, t, :], banks[t][:, 0:256], ACT.Square).then_inc(kv_out, 1)
            head_roots(0, TT * KVH, AD, 4 + 1)
            ta[0] += TT
            round_to(C_O - 1 + LEAD)
            for t in range(TT):
                if t == 0:
                    act.wait_ge(tile_done, 3)
                else:
                    act.wait_ge(chunk_used, C_O)
                for half in range(2):
                    nc.scalar.activation(xs[:, t, 512 * half:512 * half + 512], banks[2 + 2 * t + half][:, :],
                                         ACT.Square).then_inc(sq_ready, 1)
            for t in range(TT):
                head_roots(QH * t, QH, AD, 4 + 1 + t + 1)
            ta[0] += 4

            def att_round(g):
                use = ta[0] + 4 * g + 3
                act.wait_ge(turned, use + 1)
                nc.scalar.activation(ht_hi[:, 2 * g:2 * g + 2, :],
                                     turn[use % 2][:, :].rearrange("p (k t) -> p k t", k=2), ACT.Copy).then_inc(turn_hi, 1)

            for g in range(KVH):
                if g >= 2:
                    att_round(g - 2)
                act.wait_ge(negm_ready, g + 1)
                pr = prs[g % 2]
                l = banks[3 * (g % 2):3 * (g % 2) + 3]
                for hh in range(GRP):
                    nc.scalar.activation(pr[:, hh, :], l[0][:, P * hh:P * hh + P], ACT.Exp, bias=negm[:, g, 0, hh:hh + 1],
                                         accum_out=rsum[:, g, 0, hh:hh + 1])
                for hh in range(GRP):
                    ins = nc.scalar.activation(pr[:, 4 + 2 * hh:6 + 2 * hh, :].rearrange("p k c -> p (k c)"),
                                               l[1 + hh // 2][:, 256 * (hh % 2):256 * (hh % 2) + 256], ACT.Exp,
                                               bias=negm[:, g, 1, hh:hh + 1], accum_out=rsum[:, g, 1, hh:hh + 1])
                nc.scalar.activation(sinkd[:, g, :, :], sinkd[:, g, :, :], ACT.Exp).then_inc(exps_ready, 1)
            att_round(KVH - 2)
            round_to(C_O + 3)
            att_round(KVH - 1)
            ta[0] += 4 * KVH
            assert ta[0] == TURN_ATT
            round_to(C_MOE - 1 + LEAD)

            norm_stats(3)
            act.wait_ge(hn_ready, 2)
            for t in range(TT):
                nc.scalar.activation(hn_hi[:, t, :], xs[:, t, :], ACT.Copy).then_inc(hn_rounded, 1)
            ta[0] += 4
            round_to(C_MOE - 1 + ITEM_LEAD)
            act.wait_ge(gap_ready, 1)
            nc.scalar.activation(gate[:, :, 1:2], gate[:, :, 1:2], ACT.Exp).then_inc(gap_exp, 1)
            nc.scalar.activation(warm[:, :], eps[:, :], ACT.Silu)

            def gather_round(k, u):
                act.wait_ge(turned, k + 1)
                nc.scalar.activation(ht_hi[:, 4 * u:4 * u + 4, 0:P], turn[u % 2][:, :].rearrange("p (k t) -> p k t", k=4),
                                     ACT.Copy).then_inc(turn_hi, 1)

            for u in range(2):
                gather_round(ta[0], u)
                ta[0] += 1
            assert ta[0] == TURN0 and TURN0 % 2 == 0 and nxt[0] == C_MOE + ITEM_LEAD

            act.wait_ge(routed, 1)
            n_items = act.value_load(items[0:1, 16:17], min_val=E, max_val=MAX_ITEMS)
            with act.Fori(0, n_items) as n:
                for j in range(N_ITEM):
                    b, i = divmod(j, 4)
                    if b < BLK and i == 1:
                        act.wait_ge(chunk_used, n * N_ITEM + (C_MOE + j + 1))
                        act.wait_ge(hid_ready, n * BLK + (FF // 256 + max(b - 1, 0)))
                        nc.scalar.activation(e_silu[:, b % 2, :], banks[2 * (b % 2)][:, :], ACT.Silu).then_inc(silu_ready, 1)
                    hb = {4 * q + 5: q for q in range(BLK - 1)}.get(j, BLK - 1 if j == N_UP + 2 else None)
                    if hb is not None:
                        act.wait_ge(turned, n * TURN_ITEM + (TURN0 + HID_TURN[hb] + 1))
                        nc.scalar.activation(hid_hi[:, 4 * hb:4 * hb + 4, :],
                                             turn[HID_TURN[hb] % 2][:, :].rearrange("p (k t) -> p k t", k=4),
                                             ACT.Copy).then_inc(turn_hi, 1)
                    if j in (N_UP + 5, N_UP + 6):
                        u = j - N_UP - 5
                        gather_round(n * TURN_ITEM + (TURN0 + GATHER_TURN + u), u)
                    if j == N_ITEM - 1:
                        act.wait_ge(chunk_used, n * N_ITEM + (C_MOE + N_ITEM))
                        nc.scalar.activation(yb[:, 0:512], banks[4][:, :], ACT.Copy)
                        nc.scalar.activation(yb[:, 512:1024], banks[5][:, :], ACT.Copy).then_inc(yb_ready, 1)
                    c0 = C_MOE + j + ITEM_LEAD
                    round_chunk(n * N_ITEM + c0, c0 % RAW, n * (16 * N_ITEM // RAW) + 16 * (c0 // RAW + 1), c0 % SPLIT)

        @block.vector
        def _(dve):
            own = [0]
            nxt = [0]
            td = [0]

            def then(ins):
                own[0] += 1
                ins.then_inc(dve_own, 1)
                dve.wait_ge(dve_own, own[0])

            def rest_chunk(c, slot_raw, slot):
                dve.wait_ge(hi_ready, c + 1)
                nc.vector.tensor_tensor(w_lo[:, slot, :], raw[:, slot_raw, :], plain(w_hi[:, slot, :]), SUB).then_inc(split_ready, 1)

            def rest_to(c_last):
                while nxt[0] <= c_last:
                    c = nxt[0]
                    rest_chunk(c, c % RAW, c % SPLIT)
                    nxt[0] += 1

            def norm_rows(i):
                dve.wait_ge(rstd_ready, i)
                for half in range(2):
                    for t in range(TT):
                        cut = slice(512 * half, 512 * half + 512)
                        ins = nc.vector.tensor_scalar(xs[:, t, cut], h[:, t, cut], rstd[:, t:t + 1], None, MUL)
                    ins.then_inc(xs_ready, 1)

            def turn_rest(hi, lo, gain_at):
                for u in range(4):
                    dve.wait_ge(turn_hi, rounded[0] + 1)
                    bank = turn[td[0] % 2]
                    if gain_at is None:
                        nc.vector.tensor_tensor(lo[:, 2 * u:2 * u + 2, :], bank[:, :].rearrange("p (k t) -> p k t", k=2),
                                                plain(hi[:, 2 * u:2 * u + 2, :]), SUB).then_inc(turn_free, 1)
                    else:
                        for k in range(2):
                            kt = 2 * u + k
                            ins = nc.vector.scalar_tensor_tensor(
                                out=lo[:, kt, :], in0=bank[:, 256 * k:256 * k + 256],
                                scalar=cols[:, gain_at + kt:gain_at + kt + 1], in1=plain(hi[:, kt, :]), op0=MUL, op1=SUB)
                        ins.then_inc(turn_free, 1)
                    td[0] += 1
                    rounded[0] += 1

            def turn_copy(dst, part=None):
                dve.wait_ge(turned, td[0] + 1)
                src = turn[td[0] % 2][:, :] if part is None else turn[td[0] % 2][:, 0:part]
                if len(dst.shape) == 3:
                    src = src.rearrange("p (a b) -> p a b", a=dst.shape[1])
                nc.vector.tensor_copy(dst, src).then_inc(turn_free, 1)
                td[0] += 1

            def add_residual(i, c, bank_list):
                for t in range(TT):
                    if t == 0:
                        dve.wait_ge(tile_done, i)
                    else:
                        dve.wait_ge(chunk_used, c + 1)
                    for half in range(2):
                        part = h[:, t, 512 * half:512 * half + 512]
                        ins = nc.vector.tensor_tensor(part, part, bank_list[2 * t + half][:, :], ADD)
                    ins.then_inc(h_ready, 1)

            rounded = [0]
            nc.vector.memset(eps[:, :], EPS).then_inc(eps_ready, 1)
            dve.wait_ge(consts_loaded, 16 * 5)
            turn_copy(cols[:, :], 64)
            dve.wait_ge(turn_free, 1)
            l = [cols[:, 40 + 8 * i:48 + 8 * i] for i in range(3)]
            then(nc.vector.tensor_tensor(lb[:, 3, :], l[0], l[1], ALU.max))
            then(nc.vector.tensor_tensor(lb[:, 3, :], lb[:, 3, :], l[2], ALU.max))
            nc.vector.tensor_tensor(lb[:, 0:3, :], cols[:, 40:64].rearrange("p (l k) -> p l k", l=3),
                                    lb[:, 3:4, :].to_broadcast([P, 3, 8]), SUB).then_inc(lb_logit, 1)
            norm_rows(1)
            dve.wait_ge(lb_exp, 1)
            then(nc.vector.tensor_tensor(lb[:, 4, :], lb[:, 0, :], lb[:, 1, :], ADD))
            then(nc.vector.tensor_tensor(lb[:, 4, :], lb[:, 4, :], lb[:, 2, :], ADD))
            then(nc.vector.reciprocal(lb[:, 5, :], lb[:, 4, :]))
            then(nc.vector.tensor_tensor(lb[:, 6, :], lb[:, 0, :], lb[:, 5, :], MUL))
            then(nc.vector.tensor_scalar(lb[:, 7, :], lb[:, 6, :], -1.0, 1.0, MUL, ADD))
            rest_to(0)
            turn_rest(ht_hi, ht_lo, 0)
            rest_to(LEAD - 1)

            def chunks(buf):
                return buf[:, :, :].rearrange("p h (c s) -> p h c s", s=CH)

            def mask_scores(hd):
                dve.wait_ge(turned, td[0] + 1)
                if hd >= 2:
                    dve.wait_ge(o_done, hd - 1)
                nc.vector.tensor_tensor(sc[:, hd % 2, :], turn[td[0] % 2][:, 0:3 * P], const[:, K_TRI:K_TRI + 3 * P],
                                        MUL).then_inc(turn_free, 1)
                td[0] += 1

            flatT = lambda buf: buf[:, :, :].rearrange("p h t -> p (h t)")
            for c in range(N_IN):
                rest_to(c + LEAD)
                if c == 2:
                    dve.wait_ge(turned, td[0] + 1)
                    nc.vector.tensor_tensor(bias_row[:, :], turn[td[0] % 2][0:QH, 0:3 * P], const[0:QH, K_MASK:K_MASK + 3 * P],
                                            ADD).then_inc(bias_made, 1)
                    dve.wait_ge(bias_made, 1)
                    then(nc.vector.tensor_scalar(qgain[:, :], qgain[:, :], AD ** -0.5, None, MUL))
                    nc.vector.tensor_tensor(kgain[:, :], kgain[:, :], qgain[:, :], MUL).then_inc(turn_free, 1)
                    td[0] += 1
                if c < 4:
                    dve.wait_ge(proj_free, c + 1)
                    for hd in (2 * c, 2 * c + 1):
                        nc.vector.tensor_scalar(fT[:, hd, :], fT[:, hd, :], lb[:, 7, hd:hd + 1], lb[:, 6, hd:hd + 1],
                                                MUL, ADD).then_inc(f_ready, 1)
                if c == 5:
                    dve.wait_ge(ln_ready, 1)
                    nc.vector.tensor_scalar(flatT(fT), flatT(fT), -1.0, 1.0, MUL, ADD)
                    dve.wait_ge(keep_ready, 1)
                    then(nc.vector.tensor_tensor_scan(flatT(eT), xs[:, :, :].rearrange("p t d -> p (t d)"), flatT(gT),
                                                      0.0, MUL, ADD))
                if c == 6:
                    then(nc.vector.tensor_copy(mid[:, :, :], chunks(eT)[:, :, :, CH // 2 - 1]))
                    then(nc.vector.tensor_copy(tot[:, :, :], chunks(eT)[:, :, :, CH - 1]))
                    nc.vector.tensor_tensor(chunks(gT), chunks(eT), mid[:, :, :].unsqueeze(3).to_broadcast([P, HEADS, NCH, CH]),
                                            SUB).then_inc(rel_ready, 1)
                    dve.wait_ge(rel_ready, 1)
                    for i in range(1, NCH):
                        if i > 1:
                            then(nc.vector.tensor_tensor(tot[:, :, i - 1], tot[:, :, i - 1], tot[:, :, i - 2], ADD))
                        then(nc.vector.tensor_tensor(mid[:, :, i], mid[:, :, i], tot[:, :, i - 1], ADD))
                    k = 0
                    for j in range(NCH - 1):
                        for i in range(j + 1, NCH):
                            ins = nc.vector.tensor_tensor(dec[:, k, :], mid[:, :, i], mid[:, :, j], SUB)
                            k += 1
                    ins.then_inc(decays, 1)
                if c == 9:
                    dve.wait_ge(exp_ready, 1)
                    dve.wait_ge(proj_free, 8)
                    nc.vector.tensor_tensor(flatT(qT), flatT(qT), flatT(eT), MUL).then_inc(q_scaled, 1)
                if c == 11:
                    dve.wait_ge(expk_ready, 1)
                    nc.vector.tensor_tensor(flatT(fT), flatT(fT), flatT(eT), MUL)
                    dve.wait_ge(dec_ready, 1)
                    dve.wait_ge(q_scaled, 1)
                if c in (11, 12, 13):
                    j = c - 11
                    k = sum(NCH - 1 - jj for jj in range(j))
                    for i in range(j + 1, NCH):
                        ins = nc.vector.tensor_tensor(q_from[j][:, :, i - j - 1, :], chunks(qT)[:, :, i, :],
                                                      dec[:, k + i - j - 1, :].unsqueeze(2).to_broadcast([P, HEADS, CH]), MUL)
                    if c == 13:
                        ins.then_inc(hgrn_ready, 1)
                if c >= 14:
                    mask_scores(2 * (c - 14))
                    mask_scores(2 * (c - 14) + 1)
            def head_sums(n):
                b = 2 * (n % 2) + n // 2
                dve.wait_ge(sq_ready, n + 1)
                nc.vector.tensor_reduce(ssq[:, 4 * n:4 * n + 4],
                                        eT[:, 2 * b:2 * b + 2, :].rearrange("p h t -> p (h t)").rearrange("p (n e) -> p n e", e=HD),
                                        AX.X, ADD).then_inc(ssq_ready, 1)

            for hd in range(4, HEADS):
                mask_scores(hd)
                if hd in (5, 6):
                    head_sums(hd - 5)
            y = flatT(qT)
            for i in range(2):
                dve.wait_ge(root_ready, i + 1)
                part = rstd[:, 4 * TT * i:4 * TT * i + 4 * TT]
                then(nc.vector.reciprocal(part, part))
                if i == 0:
                    dve.wait_ge(og_ready, TT)
                    dve.wait_ge(o_done, HEADS)
                for hd in range(4 * i, 4 * i + 4):
                    for t in range(TT):
                        at = 4 * TT * i + 4 * t + hd % 4
                        ins = nc.vector.scalar_tensor_tensor(
                            out=y[:, D * t + HD * hd:D * t + HD * hd + HD], in0=banks[2 * t + i][:, HD * (hd % 4):HD * (hd % 4) + HD],
                            scalar=rstd[:, at:at + 1], in1=og[:, t, HD * hd:HD * hd + HD], op0=MUL, op1=MUL)
                    if hd % 2:
                        ins.then_inc(y_ready, 1)
                    if hd == 1:
                        head_sums(2)
                        head_sums(3)
            turn_rest(ht_hi, ht_lo, None)
            rest_to(C_OUT + N_OUT - 2 + LEAD)
            add_residual(1, C_FF - 1, banks[0:4])

            norm_rows(2)
            rest_to(C_FF - 1 + LEAD)
            turn_rest(ht_hi, ht_lo, 16)
            for b in range(FF // 256):
                g = C_FF + 2 * b
                rest_to(g + 1 + LEAD)
                if b >= 1:
                    dve.wait_ge(mid_rounded, b)
                    nc.vector.tensor_tensor(mid_lo[:, 2 * b - 2:2 * b, :], ff_hid[:, (b - 1) % 2, :].rearrange("p (k t) -> p k t", k=2),
                                            plain(mid_hi[:, 2 * b - 2:2 * b, :]), SUB).then_inc(mid_split, 1)
                dve.wait_ge(silu_ready, b + 1)
                dve.wait_ge(chunk_used, g + 2)
                nc.vector.tensor_tensor(ff_hid[:, b % 2, :], ff_silu[:, b % 2, :], banks[2 * (b % 2) + 1][:, :],
                                        MUL).then_inc(hid_ready, 1)
            b = FF // 256
            dve.wait_ge(mid_rounded, b)
            nc.vector.tensor_tensor(mid_lo[:, 2 * b - 2:2 * b, :], ff_hid[:, (b - 1) % 2, :].rearrange("p (k t) -> p k t", k=2),
                                    plain(mid_hi[:, 2 * b - 2:2 * b, :]), SUB).then_inc(mid_split, 1)
            rest_to(C_KV - 2 + LEAD)
            add_residual(2, C_KV - 1, [banks[4], banks[5], banks[2], banks[3]])

            norm_rows(3)
            rest_to(C_KV - 1 + LEAD)
            for u in range(4):
                dve.wait_ge(turn_hi, rounded[0] + 1)
                bank = turn[td[0] % 2]
                for hi, lo, at in ((kv_hi, kv_lo, 32), (ht_hi, ht_lo, 8)):
                    for k in range(2):
                        kt = 2 * u + k
                        ins = nc.vector.scalar_tensor_tensor(
                            out=lo[:, kt, :], in0=bank[:, 256 * k:256 * k + 256], scalar=cols[:, at + kt:at + kt + 1],
                            in1=plain(hi[:, kt, :]), op0=MUL, op1=SUB)
                ins.then_inc(turn_free, 1)
                td[0] += 1
                rounded[0] += 1
            rest_to(C_Q - 1 + LEAD)
            dve.wait_ge(kv_out, 3 * TT)
            heads = lambda ap: ap.rearrange("p (n e) -> p n e", e=AD)
            kflat = kk[:, :, :].rearrange("p t c -> p (t c)")
            nc.vector.tensor_reduce(ssq[:, 0:TT * KVH], heads(ksq[:, :, :].rearrange("p t c -> p (t c)")), AX.X, ADD).then_inc(ssq_ready, 1)
            dve.wait_ge(root_ready, 3)
            then(nc.vector.reciprocal(rstd[:, 0:TT * KVH], rstd[:, 0:TT * KVH]))
            then(nc.vector.tensor_tensor(heads(kflat), heads(kflat), rstd[:, 0:TT * KVH].unsqueeze(2).to_broadcast([P, TT * KVH, AD]), MUL))
            for i in range(2):
                nc.vector.tensor_tensor(k2[:, :, :, i, :].rearrange("p t g e -> p (t g) e"), heads(kflat),
                                        kgain[:, :].unsqueeze(1).to_broadcast([P, TT * KVH, AD]), MUL).then_inc(xs_ready, 1)
            rest_to(C_O - 2 + LEAD)
            dve.wait_ge(keys_zeroed, 1)
            for t in range(TT):
                dve.wait_ge(turned, td[0] + 1)
                for i in range(2):
                    rows = slice(AD * i, AD * i + AD)
                    ins = nc.vector.tensor_copy(kT[rows, i, :, P * t:P * t + P],
                                                turn[td[0] % 2][rows, :].rearrange("p (g c) -> p g c", g=KVH))
                ins.then_inc(turn_free, 1)
                td[0] += 1
            rest_to(C_O - 1 + LEAD)
            for t in range(TT):
                dve.wait_ge(sq_ready, 4 + 2 * t + 2)
                nc.vector.tensor_reduce(ssq[:, QH * t:QH * t + QH], heads(xs[:, t, :]), AX.X, ADD).then_inc(ssq_ready, 1)
            for t in range(TT):
                dve.wait_ge(root_ready, 4 + t)
                part = rstd[:, QH * t:QH * t + QH]
                then(nc.vector.reciprocal(part, part))
                for half in range(2):
                    n0 = QH * t + 8 * half
                    nc.vector.tensor_tensor(heads(xs[:, t, 512 * half:512 * half + 512]), heads(banks[2 + 2 * t + half][:, :]),
                                            rstd[:, n0:n0 + 8].unsqueeze(2).to_broadcast([P, 8, AD]), MUL).then_inc(xs_ready, 1)
            for t in range(TT):
                for u in range(2):
                    turn_copy(aqT[:, 4 * u:4 * u + 4, P * t:P * t + P])

            def largest(g):
                l = banks[3 * (g % 2):3 * (g % 2) + 3]
                dve.wait_ge(logits_full, 3 * g + 1)
                then(nc.vector.reduce_max(mx[:, g, 0, :], l[0][:, :].rearrange("p (h k) -> p h k", h=4), axis=AX.X))
                for i in range(2):
                    dve.wait_ge(logits_full, 3 * g + 2 + i)
                    then(nc.vector.reduce_max(mx[:, g, 1, 2 * i:2 * i + 2], l[1 + i][:, :].rearrange("p (h k) -> p h k", h=2), axis=AX.X))
                snk = sink[:, GRP * g:GRP * g + GRP].unsqueeze(1).to_broadcast([P, TT, GRP])
                then(nc.vector.tensor_tensor(mx[:, g, :, :], mx[:, g, :, :], snk, ALU.max))
                nc.vector.tensor_tensor(sinkd[:, g, :, :], snk, mx[:, g, :, :], SUB)
                nc.vector.tensor_scalar(negm[:, g, :, :], mx[:, g, :, :], -1.0, None, MUL).then_inc(negm_ready, 1)

            def normalise(g):
                pr = prs[g % 2]
                dve.wait_ge(exps_ready, g + 1)
                then(nc.vector.tensor_tensor(rsum[:, g, :, :], rsum[:, g, :, :], sinkd[:, g, :, :], ADD))
                then(nc.vector.reciprocal(rsum[:, g, :, :], rsum[:, g, :, :]))
                nc.vector.tensor_tensor(pr[:, 0:4, :], pr[:, 0:4, :], rsum[:, g, 0, :].unsqueeze(2).to_broadcast([P, 4, P]),
                                        MUL).then_inc(probs_ready, 1)
                p1 = pr[:, 4:12, :].rearrange("p (h k) c -> p h (k c)", k=2)
                nc.vector.tensor_tensor(p1, p1, rsum[:, g, 1, :].unsqueeze(2).to_broadcast([P, 4, 2 * P]), MUL).then_inc(probs_ready, 1)

            def att_rest(g):
                dve.wait_ge(turn_hi, rounded[0] + 1)
                nc.vector.tensor_tensor(ht_lo[:, 2 * g:2 * g + 2, :], turn[td[0] % 2][:, :].rearrange("p (k t) -> p k t", k=2),
                                        plain(ht_hi[:, 2 * g:2 * g + 2, :]), SUB).then_inc(turn_free, 1)
                rounded[0] += 1
                td[0] += 1

            largest(0)
            normalise(0)
            largest(1)
            for g in range(KVH):
                if g == KVH - 1:
                    rest_to(C_O + 2)
                for u in range(3):
                    turn_copy(pTs[g % 2][:, 4 * u:4 * u + 4, :])
                if g + 1 < KVH:
                    normalise(g + 1)
                if g + 2 < KVH:
                    largest(g + 2)
                if g == KVH - 1:
                    rest_to(C_O + 3)
                att_rest(g)
            rest_to(C_MOE - 2 + LEAD)
            add_residual(4, C_MOE - 1, [banks[1], banks[2], banks[4], banks[5]])

            dve.wait_ge(rstd_ready, 4)
            for half in range(2):
                for t in range(TT):
                    cut = slice(512 * half, 512 * half + 512)
                    ins = nc.vector.scalar_tensor_tensor(out=xs[:, t, cut], in0=h[:, t, cut], scalar=rstd[:, t:t + 1],
                                                         in1=gain_row[:, cut], op0=MUL, op1=MUL)
                ins.then_inc(hn_ready, 1)
            for u in range(4):
                turn_copy(hnT[:, 2 * u:2 * u + 2, :])
                if u == 1:
                    rest_to(C_MOE - 1 + LEAD)
            iota8 = const[:, K_IOTA:K_IOTA + E]
            nc.vector.memset(ones[:, :], 1.0)
            nc.vector.memset(over[:, :], 0.0)
            nc.vector.tensor_scalar(base[:, :], iota8, float(P), None, MUL)
            nc.vector.tensor_scalar(late[:, :], iota8, float(-P), float(P * (E - 1)), MUL, ADD)
            then(nc.vector.tensor_scalar(iota_p[:, :], const[0:1, K_IOTA:K_IOTA + E], 1.0 / P, None, MUL))
            dve.wait_ge(logit_full, 1)
            nc.vector.tensor_copy(lgT[:, :], banks[0][0:E, 0:T]).then_inc(lgT_ready, 1)
            dve.wait_ge(logit_full, 2)
            then(nc.vector.tensor_copy(lg[:, :, :], banks[3][:, 0:TT * E].rearrange("p (t e) -> p t e", e=E)))
            for t in range(TT):
                ins = nc.vector.max(out=top[:, t, :], in_=lg[:, t, :])
            then(ins)
            for t in range(TT):
                ins = nc.vector.max_index(out=topi[:, t, :], in_max=top[:, t, :], in_values=lg[:, t, :])
            then(ins)
            then(nc.vector.tensor_copy(topf[:, :, :], topi[:, :, 0:2]))
            every_choice = lambda ap: ap.rearrange("p t i -> p (t i)").unsqueeze(2)
            then(nc.vector.tensor_tensor(hot[:, :, :, :].rearrange("p t i e -> p (t i) e"), iota8.unsqueeze(1).to_broadcast([P, 2 * TT, E]),
                                         every_choice(topf[:, :, :]).to_broadcast([P, 2 * TT, E]), ALU.is_equal))
            nc.vector.tensor_tensor(mask[:, :, :], hot[:, :, 0, :], hot[:, :, 1, :], ADD).then_inc(mask_ready, 1)
            nc.vector.tensor_tensor(gate[:, :, 1:2], top[:, :, 1:2], top[:, :, 0:1], SUB).then_inc(gap_ready, 1)
            rest_to(C_MOE - 1 + ITEM_LEAD)
            dve.wait_ge(rank_full, 1)
            ranks = banks[1][:, 0:TT * E].rearrange("p (t e) -> p t e", e=E)
            nc.vector.tensor_scalar(over[:, 1:E + 1], banks[1][:, TT * E:TT * E + E], float(P), float(P), ALU.is_gt, MUL)
            nc.vector.tensor_scalar(big[:, :, :], ranks, float(P), None, ALU.is_ge)
            then(nc.vector.tensor_tensor(rank[:, :, :], ranks, base[:, :].unsqueeze(1).to_broadcast([P, TT, E]), ADD))
            then(nc.vector.tensor_tensor_scan(which[:, :], ones[:, :], over[:, :], 0.0, MUL, ADD))
            then(nc.vector.tensor_tensor(late[:, :], late[:, :], which[:, 0:E], ADD))
            then(nc.vector.tensor_tensor(big[:, :, :], big[:, :, :], late[:, :].unsqueeze(1).to_broadcast([P, TT, E]), MUL))
            then(nc.vector.tensor_tensor(rank[:, :, :], rank[:, :, :], big[:, :, :], ADD))
            then(nc.vector.tensor_tensor(hot[:, :, :, :], hot[:, :, :, :], rank[:, :, :].unsqueeze(2).to_broadcast([P, TT, 2, E]), MUL))
            then(nc.vector.tensor_reduce(pos[:, :, :].rearrange("p t i -> p (t i)"), hot[:, :, :, :].rearrange("p t i e -> p (t i) e"), AX.X, ADD))
            then(nc.vector.tensor_tensor(sel1[:, :, :, :].rearrange("p t i c -> p (t i) c"),
                                         const[:, K_IOTA:K_IOTA + P].unsqueeze(1).to_broadcast([P, 2 * TT, P]),
                                         every_choice(pos[:, :, :]).to_broadcast([P, 2 * TT, P]), ALU.is_equal))
            nc.vector.tensor_tensor(sel[:, :, :], sel1[:, :, 0, :], sel1[:, :, 1, :], ADD).then_inc(first_sel, 1)
            row8 = const[0:1, K_IOTA:K_IOTA + 8]
            along = lambda v: v.unsqueeze(1).to_broadcast([1, 8, E])
            nc.vector.tensor_scalar(itf[0:1, 16:17], which[0:1, E:E + 1], 1.0 / P, float(E), MUL, ADD)
            nc.vector.tensor_copy(itf[0:1, 0:8], row8)
            nc.vector.tensor_tensor(it[:, 0, :, :], along(which[0:1, 0:E]), base[0:1, :].unsqueeze(2).to_broadcast([1, 8, E]), ALU.is_equal)
            then(nc.vector.tensor_tensor(iota_p[:, :], over[0:1, 1:E + 1], iota_p[:, :], MUL))
            then(nc.vector.tensor_tensor(it[:, 1, :, :], it[:, 0, :, :], along(iota_p[:, :]), MUL))
            then(nc.vector.tensor_reduce(itf[0:1, 8:16], it[:, 1, :, :], AX.X, ADD))
            nc.vector.tensor_copy(items[0:1, 0:17], itf[0:1, 0:17])
            dve.wait_ge(gap_exp, 1)
            then(nc.vector.tensor_scalar(gate[:, :, 0:1], gate[:, :, 1:2], 1.0, None, ADD))
            then(nc.vector.reciprocal(gate[:, :, 0:1], gate[:, :, 0:1]))
            nc.vector.tensor_tensor(gate[:, :, 1:2], gate[:, :, 1:2], gate[:, :, 0:1], MUL).then_inc(routed, 1)

            def gather_rest(k_hi, u):
                dve.wait_ge(turn_hi, k_hi + 1)
                nc.vector.tensor_tensor(ht_lo[:, 4 * u:4 * u + 4, 0:P], turn[u % 2][:, :].rearrange("p (k t) -> p k t", k=4),
                                        plain(ht_hi[:, 4 * u:4 * u + 4, 0:P]), SUB).then_inc(turn_free, 1)

            for u in range(2):
                gather_rest(rounded[0], u)
                rounded[0] += 1
                td[0] += 1
            assert td[0] == TURN0 and nxt[0] == C_MOE + ITEM_LEAD
            r0 = rounded[0]

            def scatter_add(k, s):
                t, half = divmod(s, 2)
                part = h[:, t, 512 * half:512 * half + 512]
                dve.wait_ge(turned, k + 1)
                return nc.vector.tensor_tensor(part, part, turn[s % 2][:, :], ADD)

            dve.wait_ge(routed, 1)
            n_items = dve.value_load(items[0:1, 16:17], min_val=E, max_val=MAX_ITEMS)
            with dve.Fori(0, n_items) as n:
                for j in range(N_ITEM):
                    b, i = divmod(j, 4)
                    if b < BLK and i == 3:
                        dve.wait_ge(silu_ready, n * BLK + (FF // 256 + b + 1))
                        dve.wait_ge(chunk_used, n * N_ITEM + (C_MOE + j + 1))
                        nc.vector.tensor_tensor(e_hid[:, b % 2, :], e_silu[:, b % 2, :], banks[2 * (b % 2) + 1][:, :],
                                                MUL).then_inc(hid_ready, 1)
                    if 2 <= j < 6:
                        scatter_add(n * TURN_ITEM + (TURN0 + j - 2), j - 2).then_inc(turn_free, 1)
                    if j == 10:
                        dve.wait_ge(turned, n * TURN_ITEM + (TURN0 + GAT_TURN + 1))
                        nc.vector.tensor_copy(gatT[:, :], turn[GAT_TURN % 2][:, 0:T]).then_inc(turn_free, 1)
                    hb = {4 * q + 5: q for q in range(BLK - 1)}.get(j, BLK - 1 if j == N_UP + 2 else None)
                    if hb is not None:
                        dve.wait_ge(turn_hi, n * (BLK + 2) + (r0 + hb + 1))
                        nc.vector.tensor_tensor(hid_lo[:, 4 * hb:4 * hb + 4, :],
                                                turn[HID_TURN[hb] % 2][:, :].rearrange("p (k t) -> p k t", k=4),
                                                plain(hid_hi[:, 4 * hb:4 * hb + 4, :]), SUB).then_inc(turn_free, 1)
                    if j in (N_UP + 5, N_UP + 6):
                        u = j - N_UP - 5
                        gather_rest(n * (BLK + 2) + (r0 + BLK + u), u)
                    c0 = C_MOE + j + ITEM_LEAD
                    rest_chunk(n * N_ITEM + c0, c0 % RAW, c0 % SPLIT)
            for s in range(4):
                scatter_add(n_items * TURN_ITEM + (TURN0 + s), s).then_inc(turn_free, 1)

        @block.tensor
        def _(pe):
            tp = [0]
            ident = const[:, K_ID:K_ID + P]

            def product(dst, st, mv, first, last):
                nc.tensor.matmul(dst, st[0], mv[0], start=first, stop=False)
                nc.tensor.matmul(dst, st[0], mv[1], start=False, stop=False)
                return nc.tensor.matmul(dst, st[1], mv[0], start=False, stop=last)

            def turn_bank():
                if tp[0] >= 2:
                    pe.wait_ge(turn_free, tp[0] - 1)
                bank = turn[tp[0] % 2]
                tp[0] += 1
                return bank

            def turn_rows(rows, quarters=range(4)):
                for u in quarters:
                    bank = turn_bank()
                    for k in range(2):
                        for t in range(TT):
                            kt = 2 * u + k
                            ins = nc.tensor.transpose(bank[:, 256 * k + P * t:256 * k + P * t + P],
                                                      rows(t)[:, P * kt:P * kt + P], ident)
                    ins.then_inc(turned, 1)

            def turn_norm(i):
                for u in range(4):
                    pe.wait_ge(xs_ready, 2 * (i - 1) + 1 + u // 2)
                    turn_rows(lambda t: xs[:, t, :], [u])

            def split_since(since, kt):
                if since is not None and kt % 2 == 0:
                    pe.wait_ge(turn_free, since + kt // 2 + 1)

            def to_features(c, bank, hi, lo, since=None):
                pe.wait_ge(split_ready, c + 1)
                wh, wl = split_view(w_hi, c, 256), split_view(w_lo, c, 256)
                for half in range(2):
                    for k in range(KT):
                        if half == 0:
                            split_since(since, k)
                        cut = slice(P * half, P * half + P)
                        ins = product(bank[:, 256 * half:256 * half + 256], (wh[:, k, cut], wl[:, k, cut]),
                                      (hi[:, k, :], lo[:, k, :]), k == 0, k == KT - 1)
                ins.then_inc(chunk_used, 1)

            def to_rows(c, width, kts, k0, n_k, hi, lo, dst, since=None, tell=False):
                pe.wait_ge(split_ready, c + 1)
                wh, wl = split_view(w_hi, c, width), split_view(w_lo, c, width)
                for t in range(TT):
                    for q in range(max(1, width // 512)):
                        w = min(width, 512)
                        for k in range(kts):
                            kt = k0 + k
                            if t == q == 0:
                                split_since(since, kt)
                            tok = slice(P * t, P * t + P)
                            cut = slice(w * q, w * q + w)
                            ins = product(dst(t, q), (hi[:, kt, tok], lo[:, kt, tok]), (wh[:, k, cut], wl[:, k, cut]),
                                          kt == 0, kt == n_k - 1)
                    if t == 0 and tell and k0 + kts == n_k:
                        ins.then_inc(tile_done, 1)
                ins.then_inc(chunk_used, 1)

            pe.wait_ge(consts_loaded, 16 * 5)
            nc.tensor.transpose(turn_bank()[:, 0:64], vecs[:, :], const[0:64, K_ID:K_ID + 64]).then_inc(turned, 1)
            since = tp[0]
            turn_norm(1)

            def project(c):
                if 4 <= c < 12:
                    pe.wait_ge(proj_free, c - 3)
                if c >= 14:
                    pe.wait_ge(proj_free, c - 1)
                bank = proj_bank(c)
                if c < 8:
                    to_features(c, bank, ht_hi, ht_lo, since if c == 0 else None)
                else:
                    to_rows(c, 256, KT, 0, KT, ht_hi, ht_lo, lambda t, q: bank[:, 256 * t:256 * t + 256])

            for c in range(14):
                project(c)
                if c == 1:
                    pe.wait_ge(params_loaded, 16 * 8)
                    nc.tensor.matmul(turn_bank()[0:QH, 0:3 * P], rel[:, :], const[0:BUCKETS, K_HOT:K_HOT + 3 * P],
                                     start=True, stop=True).then_inc(turned, 1)
            pe.wait_ge(hgrn_ready, 1)

            def scores(hd):
                bank = turn_bank()
                score_use.append(tp[0])
                key = lambda j: fT[:, hd, CH * j:CH * j + CH]
                whole = lambda bank_rows, at, w, st, mv: nc.tensor.matmul(bank[bank_rows:bank_rows + CH, at:at + w], st, mv, start=True, stop=True)
                later = lambda j, i, n: q_from[j][:, hd, i - j - 1:i - j - 1 + n, :].rearrange("p i s -> p (i s)")
                whole(0, 0, CH, key(0), qT[:, hd, 0:CH])
                whole(0, CH, CH, key(0), later(0, 1, 1))
                whole(0, 2 * P, P, key(0), later(0, 2, 2))
                whole(CH, 0, P, key(1), qT[:, hd, 0:P])
                whole(CH, 2 * P, P, key(1), later(1, 2, 2))
                whole(0, P, CH, key(2), qT[:, hd, P:P + CH])
                whole(0, P + CH, CH, key(2), later(2, 3, 1))
                whole(CH, P, P, key(3), qT[:, hd, P:T]).then_inc(turned, 1)

            def readout(hd):
                pe.wait_ge(turn_free, score_use[hd])
                at = HD * (hd % 4)
                d0 = banks[hd // 4][:, at:at + HD]
                d1 = banks[2 + hd // 4][:, at:at + HD]
                s_ = sc[:, hd % 2, :]
                v0, v1 = (val[:, t, HD * hd:HD * hd + HD] for t in range(2))
                nc.tensor.matmul(d0, s_[:, 0:P], v0, start=True, stop=True)
                nc.tensor.matmul(d1, s_[:, 2 * P:3 * P], v0, start=True, stop=False)
                nc.tensor.matmul(d1, s_[:, P:2 * P], v1, start=False, stop=True).then_inc(o_done, 1)

            score_use = []
            scores(0)
            scores(1)
            project(14)
            readout(0)
            scores(2)
            readout(1)
            scores(3)
            project(15)
            for hd in range(2, HEADS):
                readout(hd)
                if hd + 2 < HEADS:
                    scores(hd + 2)
            since = tp[0]
            for u in range(4):
                pe.wait_ge(y_ready, u + 1)
                turn_rows(lambda t: qT[:, :, :].rearrange("p h t -> p (h t)")[:, D * t:D * t + D], [u])
            for i in range(N_OUT):
                to_rows(C_OUT + i, D, 2, 2 * i, KT, ht_hi, ht_lo, lambda t, q: banks[2 * t + q][:, :], since, True)

            since = tp[0]
            turn_norm(2)
            for b in range(FF // 256):
                if b >= 2:
                    pe.wait_ge(hid_ready, b - 1)
                for i in range(2):
                    to_features(C_FF + 2 * b + i, banks[2 * (b % 2) + i], ht_hi, ht_lo, since if b + i == 0 else None)
            down_bank = [[banks[4], banks[5]], [banks[2], banks[3]]]
            for i in range(N_DOWN):
                pe.wait_ge(mid_split, i + 1)
                to_rows(C_DOWN + i, D, 2, 2 * i, FF // P, mid_hi, mid_lo, lambda t, q: down_bank[t][q][:, :], None, True)

            logit_banks = ((0, 0, GRP), (1, 0, 2), (1, 2, GRP))

            def biases(g, b):
                t, first, last = logit_banks[b]
                nc.tensor.matmul(banks[3 * (g % 2) + b][:, :], const[:, K_ANTI:K_ANTI + P],
                                 bias_rev[:, GRP * g + first:GRP * g + last, 2 * P - P * (t + 1):2 * P],
                                 start=True, stop=False)

            since = tp[0]
            turn_norm(3)
            for i in range(N_KV):
                to_rows(C_KV + i, 512, 4, 4 * i, KT, kv_hi, kv_lo, lambda t, q: banks[t][:, :], since)
            for i in range(N_Q):
                if i == N_Q - 1:
                    pe.wait_ge(xs_ready, 3 * TT + 2)
                    for t in range(TT):
                        bank = turn_bank()
                        for g in range(KVH):
                            ins = nc.tensor.transpose(bank[:, P * g:P * g + P], k2[:, t, g, :, :].rearrange("p i e -> p (i e)"), ident)
                        ins.then_inc(turned, 1)
                to_rows(C_Q + i, D, 2, 2 * i, KT, ht_hi, ht_lo, lambda t, q: banks[2 + 2 * t + q][:, :], None, True)
            pe.wait_ge(bias_loaded, 16)
            pe.wait_ge(kv_out, 3 * TT)
            biases(0, 0)
            biases(0, 1)
            for t in range(TT):
                for u in range(2):
                    pe.wait_ge(xs_ready, 3 * TT + 2 + 2 * t + u + 1)
                    bank = turn_bank()
                    for k in range(4):
                        ins = nc.tensor.transpose(bank[:, P * k:P * k + P], xs[:, t, P * (4 * u + k):P * (4 * u + k) + P], ident)
                    ins.then_inc(turned, 1)
            queries_turned = tp[0]

            def logits(g):
                if g >= 2:
                    pe.wait_ge(exps_ready, g - 1)
                for b, (t, first, last) in enumerate(logit_banks):
                    seen = P * (t + 1)
                    if g == 0:
                        pe.wait_ge(turn_free, queries_turned - 2 * (TT - 1 - t))
                    if g > 0 or b == 2:
                        biases(g, b)
                    for hh in range(first, last):
                        head = GRP * g + hh
                        ins = nc.tensor.matmul(banks[3 * (g % 2) + b][:, seen * (hh - first):seen * (hh - first) + seen],
                                               aqT[:, head // 2, P * t:P * t + P], kT[:, hh % 2, g, 0:seen],
                                               start=False, stop=hh == last - 1)
                    ins.then_inc(logits_full, 1)

            def turn_probs(g):
                for u in range(3):
                    bank = turn_bank()
                    pe.wait_ge(probs_ready, 2 * g + (1 if u == 0 else 2))
                    for k in range(4):
                        ins = nc.tensor.transpose(bank[:, P * k:P * k + P], prs[g % 2][:, 4 * u + k, :], ident)
                    ins.then_inc(turned, 1)
                return tp[0]

            def attend(g, turned_by):
                pT = pTs[g % 2]
                pe.wait_ge(turn_free, turned_by)
                bank = turn_bank()
                for hh in range(GRP):
                    row, at = AD * (hh % 2), 256 * (hh // 2)
                    v = [vt[:, t, AD * g:AD * g + AD] for t in range(TT)]
                    d = bank[row:row + AD, at:at + 2 * P]
                    nc.tensor.matmul(d[:, 0:P], v[0], pT[:, hh, :], start=True, stop=True)
                    nc.tensor.matmul(d[:, P:2 * P], v[0], pT[:, 4 + 2 * hh, :], start=True, stop=False)
                    ins = nc.tensor.matmul(d[:, P:2 * P], v[1], pT[:, 5 + 2 * hh, :], start=False, stop=True)
                ins.then_inc(turned, 1)

            logits(0)
            logits(1)
            o_bank = [[banks[1], banks[2]], [banks[4], banks[5]]]
            attended = []

            def project_out(i):
                pe.wait_ge(turn_free, attended[i])
                to_rows(C_O + i, D, 2, 2 * i, KT, ht_hi, ht_lo, lambda t, q: o_bank[t][q][:, :], None, True)

            for g in range(KVH):
                turned_by = turn_probs(g)
                if g + 2 < KVH:
                    logits(g + 2)
                if g == KVH - 1:
                    project_out(1)
                attend(g, turned_by)
                attended.append(tp[0])
                if g == KVH - 2:
                    pe.wait_ge(exps_ready, KVH)
                    project_out(0)
            assert tp[0] == TURN_ATT
            for i in range(2, N_O):
                project_out(i)

            since = tp[0]
            for u in range(4 + 1):
                if u < 4:
                    pe.wait_ge(hn_ready, 1 + u // 2)
                    turn_rows(lambda t: xs[:, t, :], [u])
                if u >= 1:
                    pe.wait_ge(turn_free, since + u)
                    for k in (2 * u - 2, 2 * u - 1):
                        ins = nc.tensor.matmul(banks[0][0:E, 0:T], router[:, k, :], hnT[:, k, :],
                                               start=k == 0, stop=k == KT - 1)
            ins.then_inc(logit_full, 1)
            pe.wait_ge(lgT_ready, 1)
            for t in range(TT):
                ins = nc.tensor.transpose(banks[3][:, E * t:E * t + E], lgT[:, P * t:P * t + P], const[0:E, K_ID:K_ID + E])
            ins.then_inc(logit_full, 1)
            pe.wait_ge(mask_ready, 1)
            before, every = const[:, K_STRICT:K_STRICT + P], const[:, K_TRI + 2 * P:K_TRI + 3 * P]
            m = [mask[:, t, :] for t in range(TT)]
            r = [banks[1][:, E * i:E * i + E] for i in range(3)]
            nc.tensor.matmul(r[0], before, m[0], start=True, stop=True)
            nc.tensor.matmul(r[1], every, m[0], start=True, stop=False)
            nc.tensor.matmul(r[1], before, m[1], start=False, stop=True)
            nc.tensor.matmul(r[2], every, m[0], start=True, stop=False)
            nc.tensor.matmul(r[2], every, m[1], start=False, stop=True).then_inc(rank_full, 1)

            def gather(u):
                for k in range(4):
                    kt = 4 * u + k
                    for t in range(TT):
                        for i, part in enumerate((hn_hi, hn_lo)):
                            ins = nc.tensor.matmul(turn[u % 2][:, P * k:P * k + P], part[:, t, P * kt:P * kt + P], sel[:, t, :],
                                                   start=t + i == 0, stop=t + i == 2)
                ins.then_inc(turned, 1)

            def scatter(s):
                t, half = divmod(s, 2)
                nc.tensor.matmul(turn[s % 2][:, :], gatT[:, P * t:P * t + P], yb[:, 512 * half:512 * half + 512],
                                 start=True, stop=True).then_inc(turned, 1)

            pe.wait_ge(hn_split, TT)
            pe.wait_ge(first_sel, 1)
            for u in range(2):
                turn_bank()
                gather(u)
            assert tp[0] == TURN0

            pe.wait_ge(routed, 1)
            n_items = pe.value_load(items[0:1, 16:17], min_val=E, max_val=MAX_ITEMS)
            with pe.Fori(0, n_items) as n:
                def free_turn(i):
                    pe.wait_ge(turn_free, n * TURN_ITEM + (TURN0 + i - 1))

                for j in range(N_ITEM):
                    c0 = C_MOE + j
                    b, i = divmod(j, 4)
                    if j < 2:
                        pe.wait_ge(turn_free, n * TURN_ITEM + (TURN0 - 1 + j))
                    if j < N_UP and i == 0:
                        pe.wait_ge(hid_ready, n * BLK + (FF // 256 + max(b - 1, 0)))
                    if j >= N_UP:
                        d = j - N_UP
                        if d % 2 == 0:
                            pe.wait_ge(turn_free, n * TURN_ITEM + (TURN0 + HID_TURN[d // 2] + 1))
                    pe.wait_ge(split_ready, n * N_ITEM + (c0 + 1))
                    if j < N_UP:
                        wh, wl = split_view(w_hi, c0, 512), split_view(w_lo, c0, 512)
                        bank = banks[2 * (b % 2) + i // 2]
                        for k in range(4):
                            kt = 4 * (i % 2) + k
                            ins = product(bank[:, :], (ht_hi[:, kt, 0:P], ht_lo[:, kt, 0:P]), (wh[:, k, :], wl[:, k, :]),
                                          kt == 0, kt == KT - 1)
                    else:
                        wh, wl = split_view(w_hi, c0, D), split_view(w_lo, c0, D)
                        for k in range(2):
                            kt = 2 * d + k
                            for q in range(2):
                                cut = slice(512 * q, 512 * q + 512)
                                ins = product(banks[4 + q][:, :], (hid_hi[:, kt, :], hid_lo[:, kt, :]),
                                              (wh[:, k, cut], wl[:, k, cut]), kt == 0, kt == FKT - 1)
                    ins.then_inc(chunk_used, 1)
                    if 2 <= j < 6:
                        s_ = j - 2
                        if s_ == 0:
                            pe.wait_ge(yb_ready, n + 1)
                        free_turn(s_)
                        scatter(s_)
                    if j == 10:
                        pe.wait_ge(sel_ready, n + 1)
                        free_turn(GAT_TURN)
                        for t in range(TT):
                            ins = nc.tensor.transpose(turn[GAT_TURN % 2][:, P * t:P * t + P], gat[:, t, :], ident)
                        ins.then_inc(turned, 1)
                    hb = {4 * q + 5: q for q in range(BLK - 1)}.get(j, BLK - 1 if j == N_UP + 2 else None)
                    if hb is not None:
                        pe.wait_ge(hid_ready, n * BLK + (FF // 256 + hb + 1))
                        free_turn(HID_TURN[hb])
                        for k in range(4):
                            ins = nc.tensor.transpose(turn[HID_TURN[hb] % 2][:, P * k:P * k + P],
                                                      e_hid[:, hb % 2, P * k:P * k + P], ident)
                        ins.then_inc(turned, 1)
                    if j in (N_UP + 5, N_UP + 6):
                        u = j - N_UP - 5
                        pe.wait_ge(sel_ready, n + 2)
                        free_turn(GATHER_TURN + u)
                        gather(u)
            for s_ in range(4):
                pe.wait_ge(turn_free, n_items * TURN_ITEM + (TURN0 + s_ - 1))
                if s_ == 0:
                    pe.wait_ge(yb_ready, n_items + 1)
                scatter(s_)


_INS = ["x", "hgrn_w_in", "hgrn_lb", "hgrn_gnorm", "hgrn_w_out", "swa_w_q", "swa_q_gain", "swa_sink", "swa_w_o",
        "kv_norm", "kv_w", "k_gain", "rel_bias", "attn_norm", "ffn_norm", "ffn_w_gate", "ffn_w_up", "ffn_w_down",
        "moe_router", "moe_w_gate", "moe_w_up", "moe_w_down"]


def kernel(**inputs):
    import concourse.bacc as bacc
    from concourse.bass_utils import run_bass_kernel_spmd

    nc = bacc.Bacc("TRN2", target_bir_lowering=False, num_devices=1)
    arrays = {name: np.ascontiguousarray(inputs[name]) for name in _INS}
    arrays["shape_constants"] = shape_constants()
    aps = {name: nc.dram_tensor(f"in_{name}", v.shape, mybir.dt.from_np(v.dtype), kind="ExternalInput").ap()
           for name, v in arrays.items()}
    out = nc.dram_tensor("out", (1, T, D), mybir.dt.float32, kind="ExternalOutput").ap()
    build_program(nc, aps, out)
    r = run_bass_kernel_spmd(nc, [{f"in_{k}": v for k, v in arrays.items()}], core_ids=[0])
    return r.results[0]["out"]
```
